# Optimizing a Trainium2 kernel written in Bass

```python
import math
import jax, jax.numpy as jnp
from jax import lax
import numpy as np

D_MODEL = 1024
BATCH = 1
SEQ = 512
DEPTH = 1

PLE_DIM = 256
D_FF = 2816
EPS = 1e-6
ATT_HEADS = 8
ATT_HEAD_DIM = 64
KV_LATENT = 128
IDX_HEADS = 8
IDX_HEAD_DIM = 64
TOPK_MAX = 256
Q_BLOCK = 128
ATT_SCALE = ATT_HEAD_DIM ** -0.5
IDX_W_SCALE = (IDX_HEADS ** -0.5) * (IDX_HEAD_DIM ** -0.5)
REL_BUCKETS = 32
REL_MAX_DIST = 128
HG_HEADS = 4
HG_KEY_DIM = 128
HG_VAL_DIM = 128
CHUNK = 64
ATT_WIDTH = ATT_HEADS * ATT_HEAD_DIM
IDX_Q_WIDTH = IDX_HEADS * IDX_HEAD_DIM
HG_KW = HG_HEADS * HG_KEY_DIM
HG_VW = HG_HEADS * HG_VAL_DIM
IN_SPLITS = (ATT_WIDTH, KV_LATENT, IDX_Q_WIDTH, IDX_HEAD_DIM, IDX_HEADS, HG_KW, HG_KW, HG_VW, HG_VW, D_MODEL, D_MODEL)
N_IN = sum(IN_SPLITS)


def rms_norm(x, g):
    xf = x.astype(jnp.float32)
    y = xf * lax.rsqrt(jnp.mean(xf * xf, axis=-1, keepdims=True) + EPS)
    return (y * g.astype(jnp.float32)).astype(x.dtype)

def swiglu(x, w_gate, w_up, w_down):
    return (jax.nn.silu(x @ w_gate) * (x @ w_up)) @ w_down

def split_cols(a):
    outs = []
    off = 0
    for w in IN_SPLITS:
        outs.append(a[..., off:off + w])
        off += w
    return outs

def rel_bucket(dist):
    max_exact = REL_BUCKETS // 2
    d_f = jnp.maximum(dist, 1).astype(jnp.float32)
    log_b = max_exact + (jnp.log(d_f / max_exact) / math.log(REL_MAX_DIST / max_exact)
                         * (REL_BUCKETS - max_exact)).astype(jnp.int32)
    return jnp.where(dist < max_exact, dist, jnp.minimum(log_b, REL_BUCKETS - 1))

def dsa_branch(q, c_kv, q_idx, k_idx, w_idx, w_uk, w_uv, rel_bias):
    B_, S_ = q.shape[0], q.shape[1]
    topk = min(TOPK_MAX, S_ // 4)
    nblk = S_ // Q_BLOCK
    q_lat = jnp.einsum('bshd,hcd->bshc', q, w_uk)
    key_pos = jnp.arange(S_, dtype=jnp.int32)

    def to_blocks(a):
        return jnp.moveaxis(a.reshape((B_, nblk, Q_BLOCK) + a.shape[2:]), 1, 0)

    def block(args):
        ql, qi, wi, t_pos = args
        dots = jnp.einsum('bqhd,bsd->bqhs', qi, k_idx)
        score = jnp.einsum('bqh,bqhs->bqs', wi, jax.nn.relu(dots)).astype(jnp.float32)
        causal = key_pos[None, :] <= t_pos[:, None]
        score = jnp.where(causal[None], score, -jnp.inf)
        _, idx = lax.top_k(score, topk)
        valid = idx <= t_pos[None, :, None]
        c_sel = jax.vmap(lambda c, i: c[i])(c_kv, idx)
        dist = jnp.maximum(t_pos[None, :, None] - idx, 0)
        bias = jnp.moveaxis(rel_bias[rel_bucket(dist)], -1, 2)
        logits = (jnp.einsum('bqhc,bqkc->bqhk', ql.astype(jnp.float32), c_sel.astype(jnp.float32)) * ATT_SCALE
                  + bias.astype(jnp.float32))
        logits = jnp.where(valid[:, :, None, :], logits, -jnp.inf)
        probs = jax.nn.softmax(logits, axis=-1).astype(c_kv.dtype)
        return jnp.einsum('bqhk,bqkc->bqhc', probs, c_sel)

    t_blocks = jnp.arange(S_, dtype=jnp.int32).reshape(nblk, Q_BLOCK)
    o_lat = lax.map(block, (to_blocks(q_lat), to_blocks(q_idx), to_blocks(w_idx), t_blocks))
    o_lat = jnp.moveaxis(o_lat, 0, 1).reshape(B_, S_, ATT_HEADS, KV_LATENT)
    o = jnp.einsum('bshc,hcd->bshd', o_lat, w_uv)
    return o.reshape(B_, S_, ATT_WIDTH)

def hgrn2_chunkwise(q, k, v, log_f):
    B_, S_, H_, DK_ = q.shape
    DV_ = v.shape[-1]
    n = S_ // CHUNK

    def chunks(a):
        return jnp.moveaxis(a.astype(jnp.float32).reshape(B_, n, CHUNK, H_, a.shape[-1]), 1, 0)

    tri = jnp.tril(jnp.ones((CHUNK, CHUNK), dtype=bool))

    def step(state, inp):
        qc, kc, vc, gc = inp
        G = jnp.cumsum(gc, axis=1)
        o_inter = jnp.einsum('bthk,bhkv->bthv', qc * jnp.exp(G), state)
        diff = G[:, :, None] - G[:, None, :]
        decay = jnp.exp(jnp.where(tri[None, :, :, None, None], diff, -jnp.inf))
        A = jnp.einsum('bthk,bshk,btshk->bhts', qc, kc, decay)
        o_intra = jnp.einsum('bhts,bshv->bthv', A, vc)
        G_last = G[:, -1]
        k_dec = kc * jnp.exp(G_last[:, None] - G)
        new_state = jnp.exp(G_last)[..., None] * state + jnp.einsum('bshk,bshv->bhkv', k_dec, vc)
        return new_state, o_inter + o_intra

    s0 = jnp.zeros((B_, H_, DK_, DV_), jnp.float32)
    _, o = lax.scan(step, s0, (chunks(q), chunks(k), chunks(v), chunks(log_f)))
    return jnp.moveaxis(o, 0, 1).reshape(B_, S_, H_, DV_)

def first_inputs(seed: int = 0) -> dict:
    key = jax.random.key(seed)
    ks = jax.random.split(key, 40)

    def nrm(k, shape, scale):
        return jax.random.normal(k, shape, jnp.float32) * scale

    def gain(k, shape):
        return 1.0 + 0.05 * jax.random.normal(k, shape, jnp.float32)

    L = DEPTH
    D = D_MODEL
    return {
        'x': nrm(ks[0], (BATCH, SEQ, D), 1.0),
        'p': nrm(ks[1], (DEPTH, BATCH, SEQ, PLE_DIM), 1.0),
        'rel_bias': nrm(ks[2], (REL_BUCKETS, ATT_HEADS), 0.1),
        'hgrn_lb': nrm(ks[3], (DEPTH + 1, HG_KW), 1.0),
        'ffn1_pre_g': gain(ks[4], (L, D)),
        'ffn1_post_g': gain(ks[5], (L, D)),
        'ffn1_w_gate': nrm(ks[6], (L, D, D_FF), D ** -0.5),
        'ffn1_w_up': nrm(ks[7], (L, D, D_FF), D ** -0.5),
        'ffn1_w_down': nrm(ks[8], (L, D_FF, D), D_FF ** -0.5),
        'mix_pre_g': gain(ks[9], (L, D)),
        'mix_post_g': gain(ks[10], (L, D)),
        'w_in': nrm(ks[11], (L, D, N_IN), D ** -0.5),
        'kv_norm_g': gain(ks[12], (L, KV_LATENT)),
        'kidx_norm_g': gain(ks[13], (L, IDX_HEAD_DIM)),
        'w_uk': nrm(ks[14], (L, ATT_HEADS, KV_LATENT, ATT_HEAD_DIM), KV_LATENT ** -0.5),
        'w_uv': nrm(ks[15], (L, ATT_HEADS, KV_LATENT, ATT_HEAD_DIM), KV_LATENT ** -0.5),
        'hgrn_norm_g': gain(ks[16], (L, HG_VAL_DIM)),
        'w_br_a': nrm(ks[17], (L, ATT_WIDTH, D), ATT_WIDTH ** -0.5),
        'w_br_b': nrm(ks[18], (L, HG_VW, D), HG_VW ** -0.5),
        'b_gate': nrm(ks[19], (L, 2 * D), 0.02),
        'w_out': nrm(ks[20], (L, D, D), D ** -0.5),
        'ffn2_pre_g': gain(ks[21], (L, D)),
        'ffn2_post_g': gain(ks[22], (L, D)),
        'ffn2_w_gate': nrm(ks[23], (L, D, D_FF), D ** -0.5),
        'ffn2_w_up': nrm(ks[24], (L, D, D_FF), D ** -0.5),
        'ffn2_w_down': nrm(ks[25], (L, D_FF, D), D_FF ** -0.5),
        'ple_pre_g': gain(ks[26], (L, D)),
        'ple_post_g': gain(ks[27], (L, D)),
        'w_ple_gate': nrm(ks[28], (L, D, D), D ** -0.5),
        'w_ple_proj': nrm(ks[29], (L, PLE_DIM, D), PLE_DIM ** -0.5),
    }

def first_block(x, p, rel_bias, hgrn_lb, ffn1_pre_g, ffn1_post_g, ffn1_w_gate, ffn1_w_up, ffn1_w_down,
              mix_pre_g, mix_post_g, w_in, kv_norm_g, kidx_norm_g, w_uk, w_uv, hgrn_norm_g,
              w_br_a, w_br_b, b_gate, w_out, ffn2_pre_g, ffn2_post_g, ffn2_w_gate, ffn2_w_up, ffn2_w_down,
              ple_pre_g, ple_post_g, w_ple_gate, w_ple_proj):
    B_, S_, D = x.shape
    lower_bounds = jnp.cumsum(jax.nn.softmax(hgrn_lb.astype(jnp.float32), axis=0), axis=0)
    h = x
    for i in range(DEPTH):
        h = h + 0.5 * rms_norm(swiglu(rms_norm(h, ffn1_pre_g[i]), ffn1_w_gate[i], ffn1_w_up[i], ffn1_w_down[i]),
                               ffn1_post_g[i])
        u = rms_norm(h, mix_pre_g[i])
        proj = u @ w_in[i]
        (q_a, c_kv, q_idx, k_idx, w_idx, q_h, f_h, i_h, g_h, gate_a, gate_b) = split_cols(proj)
        c_kv = rms_norm(c_kv, kv_norm_g[i])
        k_idx = rms_norm(k_idx, kidx_norm_g[i])
        y_a = dsa_branch(q_a.reshape(B_, S_, ATT_HEADS, ATT_HEAD_DIM), c_kv,
                         q_idx.reshape(B_, S_, IDX_HEADS, IDX_HEAD_DIM), k_idx, w_idx * IDX_W_SCALE,
                         w_uk[i], w_uv[i], rel_bias)
        lb = lower_bounds[i]
        f = (lb + (1.0 - lb) * jax.nn.sigmoid(f_h.astype(jnp.float32))).reshape(B_, S_, HG_HEADS, HG_KEY_DIM)
        o_h = hgrn2_chunkwise(jax.nn.silu(q_h).reshape(B_, S_, HG_HEADS, HG_KEY_DIM), 1.0 - f,
                              i_h.reshape(B_, S_, HG_HEADS, HG_VAL_DIM), jnp.log(f))
        o_h = rms_norm(o_h, hgrn_norm_g[i]) * jax.nn.silu(g_h.astype(jnp.float32).reshape(B_, S_, HG_HEADS, HG_VAL_DIM))
        y_b = o_h.reshape(B_, S_, HG_VW).astype(x.dtype)
        merged = (jax.nn.sigmoid(gate_a + b_gate[i, :D]) * (y_a @ w_br_a[i])
                  + jax.nn.sigmoid(gate_b + b_gate[i, D:]) * (y_b @ w_br_b[i]))
        h = h + rms_norm(merged @ w_out[i], mix_post_g[i])
        h = h + 0.5 * rms_norm(swiglu(rms_norm(h, ffn2_pre_g[i]), ffn2_w_gate[i], ffn2_w_up[i], ffn2_w_down[i]),
                               ffn2_post_g[i])
        ple_gate = jax.nn.sigmoid(rms_norm(h, ple_pre_g[i]) @ w_ple_gate[i])
        h = h + rms_norm(ple_gate * (p[i] @ w_ple_proj[i]), ple_post_g[i])
    return h


DEPTH_2 = 2

N_A_LAYERS = max(1, DEPTH_2 // 2)
N_B_LAYERS = DEPTH_2 - N_A_LAYERS

DIFF_HEADS = 8
DIFF_QK_DIM = 64
DIFF_V_DIM = 2 * DIFF_QK_DIM
T5_BUCKETS = 32
T5_MAX_DISTANCE = 128
MLA_HEADS = 16
MLA_QK_NOPE = 128
MLA_QK_ROPE = 64
MLA_V_DIM = 128
MLA_Q_LORA = 512
MLA_KV_LORA = 256
ROPE_BASE = 10000.0
CONV_WIDTH = 3
RMS_EPS = 1e-6
NEG_INF = -1e30
POS_OFFSET_MAX = 1024


def rms_norm_2(x, gain):
    xf = x.astype(jnp.float32)
    y = xf * lax.rsqrt(jnp.mean(xf * xf, axis=-1, keepdims=True) + RMS_EPS)
    return (y * gain.astype(jnp.float32)).astype(x.dtype)

def rotary(x, pos):
    d = x.shape[-1]
    half = d // 2
    inv_freq = jnp.exp(-math.log(ROPE_BASE) * jnp.arange(half, dtype=jnp.float32) * (2.0 / d))
    ang = pos.astype(jnp.float32)[..., None] * inv_freq
    if x.ndim == 4:
        ang = ang[:, :, None, :]
    cos, sin = jnp.cos(ang), jnp.sin(ang)
    xf = x.astype(jnp.float32)
    x1, x2 = xf[..., :half], xf[..., half:]
    return jnp.concatenate([x1 * cos - x2 * sin, x1 * sin + x2 * cos], axis=-1).astype(x.dtype)

def t5_bucket(dist):
    n = jnp.maximum(dist, 0)
    max_exact = T5_BUCKETS // 2
    log_ratio = jnp.log(jnp.maximum(n, 1).astype(jnp.float32) / max_exact) / math.log(T5_MAX_DISTANCE / max_exact)
    large = max_exact + (log_ratio * (T5_BUCKETS - max_exact)).astype(jnp.int32)
    large = jnp.minimum(large, T5_BUCKETS - 1)
    return jnp.where(n < max_exact, n, large)

def to_blocks(t):
    b, s = t.shape[:2]
    return t.reshape((b, s // Q_BLOCK, Q_BLOCK) + t.shape[2:]).swapaxes(0, 1)

def from_blocks(t):
    nb, b, q = t.shape[:3]
    return t.swapaxes(0, 1).reshape((b, nb * q) + t.shape[3:])

def causal_mask(blk_idx, seq):
    q_idx = blk_idx * Q_BLOCK + jnp.arange(Q_BLOCK)
    return jnp.arange(seq)[None, :] <= q_idx[:, None]

def diff_attention(h, pos, w_qkv, q_gain, k_gain, lam_q1, lam_k1, lam_q2, lam_k2, sub_gain, w_o, rel_table, lam_init):
    b, s, _ = h.shape
    qk_w = DIFF_HEADS * 2 * DIFF_QK_DIM
    qkv = h @ w_qkv
    q = rms_norm_2(qkv[..., :qk_w].reshape(b, s, DIFF_HEADS, 2, DIFF_QK_DIM), q_gain)
    k = rms_norm_2(qkv[..., qk_w:2 * qk_w].reshape(b, s, DIFF_HEADS, 2, DIFF_QK_DIM), k_gain)
    v = qkv[..., 2 * qk_w:].reshape(b, s, DIFF_HEADS, DIFF_V_DIM)
    f32 = jnp.float32
    lam = (jnp.exp(jnp.sum(lam_q1.astype(f32) * lam_k1.astype(f32)))
           - jnp.exp(jnp.sum(lam_q2.astype(f32) * lam_k2.astype(f32))) + lam_init)
    scale = DIFF_QK_DIM ** -0.5
    nb = s // Q_BLOCK

    def block(args):
        i, q_blk, p_blk = args
        sc = jnp.einsum('bqhcd,bkhcd->bhcqk', q_blk, k).astype(f32) * scale
        bucket = t5_bucket(p_blk[:, :, None] - pos[:, None, :])
        bias = jnp.take(rel_table, bucket, axis=0).astype(f32)
        bias = bias.transpose(0, 3, 1, 2)[:, :, None]
        sc = jnp.where(causal_mask(i, s), sc + bias, NEG_INF)
        a = jax.nn.softmax(sc, axis=-1)
        wts = a[:, :, 0] - lam * a[:, :, 1]
        return jnp.einsum('bhqk,bkhv->bqhv', wts.astype(v.dtype), v)

    o = lax.map(block, (jnp.arange(nb), to_blocks(q), to_blocks(pos)))
    o = from_blocks(o)
    o = rms_norm_2(o, sub_gain) * (1.0 - lam_init)
    return o.reshape(b, s, DIFF_HEADS * DIFF_V_DIM) @ w_o

def shared_latent_kv(h, pos, kv_norm, w_dkv, ckv_norm, w_ukv, k_nope_norm, k_pe_norm):
    b, s, _ = h.shape
    hn = rms_norm_2(h, kv_norm)
    ckv_full = hn @ w_dkv
    c_kv = rms_norm_2(ckv_full[..., :MLA_KV_LORA], ckv_norm)
    k_pe = rotary(rms_norm_2(ckv_full[..., MLA_KV_LORA:], k_pe_norm), pos)
    kv = (c_kv @ w_ukv).reshape(b, s, MLA_HEADS, MLA_QK_NOPE + MLA_V_DIM)
    k_nope = rms_norm_2(kv[..., :MLA_QK_NOPE], k_nope_norm)
    v = kv[..., MLA_QK_NOPE:]
    return k_nope, k_pe, v

def mla_attention(h, pos, w_dq, cq_norm, w_uq, q_nope_norm, q_pe_norm, w_o, k_nope, k_pe, v):
    b, s, _ = h.shape
    c_q = rms_norm_2(h @ w_dq, cq_norm)
    q = (c_q @ w_uq).reshape(b, s, MLA_HEADS, MLA_QK_NOPE + MLA_QK_ROPE)
    q_nope = rms_norm_2(q[..., :MLA_QK_NOPE], q_nope_norm)
    q_pe = rotary(rms_norm_2(q[..., MLA_QK_NOPE:], q_pe_norm), pos)
    scale = (MLA_QK_NOPE + MLA_QK_ROPE) ** -0.5
    nb = s // Q_BLOCK

    def block(args):
        i, qn, qp = args
        sc = (jnp.einsum('bqhd,bkhd->bhqk', qn, k_nope)
              + jnp.einsum('bqhr,bkr->bhqk', qp, k_pe)).astype(jnp.float32) * scale
        sc = jnp.where(causal_mask(i, s), sc, NEG_INF)
        a = jax.nn.softmax(sc, axis=-1)
        return jnp.einsum('bhqk,bkhv->bqhv', a.astype(v.dtype), v)

    o = from_blocks(lax.map(block, (jnp.arange(nb), to_blocks(q_nope), to_blocks(q_pe))))
    return o.reshape(b, s, MLA_HEADS * MLA_V_DIM) @ w_o

def conv_gated_ffn(h, w_in, conv_w, conv_b, w_out):
    s = h.shape[1]
    u = h @ w_in
    u_pad = jnp.pad(u, ((0, 0), (CONV_WIDTH - 1, 0), (0, 0)))
    c = conv_b
    for j in range(CONV_WIDTH):
        c = c + u_pad[:, j:j + s, :] * conv_w[j]
    a, g = jnp.split(c, 2, axis=-1)
    return (jax.nn.silu(g) * a) @ w_out

def per_layer_embedding(h, p_i, norm_g, w_proj, w_gate):
    gate = jax.nn.sigmoid(rms_norm_2(h, norm_g) @ w_gate)
    return (p_i @ w_proj) * gate

def second_inputs(seed: int = 0) -> dict:
    key = jax.random.key(seed)
    keys = iter(jax.random.split(key, 48))
    f32 = jnp.float32

    def dense(shape, fan_in):
        return jax.random.normal(next(keys), shape, f32) * fan_in ** -0.5

    def gain(shape):
        return 1.0 + 0.05 * jax.random.normal(next(keys), shape, f32)

    def small(shape, scale):
        return scale * jax.random.normal(next(keys), shape, f32)

    na, nbl = N_A_LAYERS, N_B_LAYERS
    qkv_w = 2 * DIFF_HEADS * 2 * DIFF_QK_DIM + DIFF_HEADS * DIFF_V_DIM
    x = jax.random.normal(next(keys), (BATCH, SEQ, D_MODEL), f32)
    p = jax.random.normal(next(keys), (DEPTH_2, BATCH, SEQ, PLE_DIM), f32)
    offsets = jax.random.randint(next(keys), (BATCH, 1), 0, POS_OFFSET_MAX, dtype=jnp.int32)
    positions = offsets + jnp.arange(SEQ, dtype=jnp.int32)[None, :]
    return {
        'x': x,
        'p': p,
        'positions': positions,
        'rel_bias_table': small((T5_BUCKETS, DIFF_HEADS), 0.5),
        'attn_norm': gain((DEPTH_2, D_MODEL)),
        'a_w_qkv': dense((na, D_MODEL, qkv_w), D_MODEL),
        'a_q_norm': gain((na, DIFF_QK_DIM)),
        'a_k_norm': gain((na, DIFF_QK_DIM)),
        'a_lam_q1': small((na, DIFF_QK_DIM), 0.1),
        'a_lam_k1': small((na, DIFF_QK_DIM), 0.1),
        'a_lam_q2': small((na, DIFF_QK_DIM), 0.1),
        'a_lam_k2': small((na, DIFF_QK_DIM), 0.1),
        'a_sub_norm': gain((na, DIFF_V_DIM)),
        'a_w_o': dense((na, DIFF_HEADS * DIFF_V_DIM, D_MODEL), DIFF_HEADS * DIFF_V_DIM),
        'kv_norm': gain((D_MODEL,)),
        'w_dkv': dense((D_MODEL, MLA_KV_LORA + MLA_QK_ROPE), D_MODEL),
        'ckv_norm': gain((MLA_KV_LORA,)),
        'w_ukv': dense((MLA_KV_LORA, MLA_HEADS * (MLA_QK_NOPE + MLA_V_DIM)), MLA_KV_LORA),
        'k_nope_norm': gain((MLA_QK_NOPE,)),
        'k_pe_norm': gain((MLA_QK_ROPE,)),
        'b_w_dq': dense((nbl, D_MODEL, MLA_Q_LORA), D_MODEL),
        'b_cq_norm': gain((nbl, MLA_Q_LORA)),
        'b_w_uq': dense((nbl, MLA_Q_LORA, MLA_HEADS * (MLA_QK_NOPE + MLA_QK_ROPE)), MLA_Q_LORA),
        'b_q_nope_norm': gain((nbl, MLA_QK_NOPE)),
        'b_q_pe_norm': gain((nbl, MLA_QK_ROPE)),
        'b_w_o': dense((nbl, MLA_HEADS * MLA_V_DIM, D_MODEL), MLA_HEADS * MLA_V_DIM),
        'ffn_norm': gain((DEPTH_2, D_MODEL)),
        'ffn_w_in': dense((DEPTH_2, D_MODEL, 2 * D_FF), D_MODEL),
        'ffn_conv_w': dense((DEPTH_2, CONV_WIDTH, 2 * D_FF), CONV_WIDTH),
        'ffn_conv_b': small((DEPTH_2, 2 * D_FF), 0.02),
        'ffn_w_out': dense((DEPTH_2, D_FF, D_MODEL), D_FF),
        'ple_norm': gain((DEPTH_2, D_MODEL)),
        'ple_w_proj': dense((DEPTH_2, PLE_DIM, D_MODEL), PLE_DIM),
        'ple_w_gate': dense((DEPTH_2, D_MODEL, D_MODEL), D_MODEL),
    }

def second_block(x, p, positions, rel_bias_table, attn_norm,
              a_w_qkv, a_q_norm, a_k_norm, a_lam_q1, a_lam_k1, a_lam_q2, a_lam_k2, a_sub_norm, a_w_o,
              kv_norm, w_dkv, ckv_norm, w_ukv, k_nope_norm, k_pe_norm,
              b_w_dq, b_cq_norm, b_w_uq, b_q_nope_norm, b_q_pe_norm, b_w_o,
              ffn_norm, ffn_w_in, ffn_conv_w, ffn_conv_b, ffn_w_out,
              ple_norm, ple_w_proj, ple_w_gate):
    h = x
    shared = None
    for i in range(DEPTH_2):
        hn = rms_norm_2(h, attn_norm[i])
        if i < N_A_LAYERS:
            lam_init = 0.8 - 0.6 * math.exp(-0.3 * i)
            mix = diff_attention(hn, positions, a_w_qkv[i], a_q_norm[i], a_k_norm[i],
                                 a_lam_q1[i], a_lam_k1[i], a_lam_q2[i], a_lam_k2[i],
                                 a_sub_norm[i], a_w_o[i], rel_bias_table, lam_init)
        else:
            if shared is None:
                shared = shared_latent_kv(h, positions, kv_norm, w_dkv, ckv_norm, w_ukv,
                                          k_nope_norm, k_pe_norm)
            j = i - N_A_LAYERS
            k_nope, k_pe, v = shared
            mix = mla_attention(hn, positions, b_w_dq[j], b_cq_norm[j], b_w_uq[j],
                                b_q_nope_norm[j], b_q_pe_norm[j], b_w_o[j], k_nope, k_pe, v)
        h = h + mix
        h = h + conv_gated_ffn(rms_norm_2(h, ffn_norm[i]), ffn_w_in[i], ffn_conv_w[i],
                               ffn_conv_b[i], ffn_w_out[i])
        h = h + per_layer_embedding(h, p[i], ple_norm[i], ple_w_proj[i], ple_w_gate[i])
    return h


def setup_inputs(seed=0):
    out = dict(first_inputs(seed))
    for name, value in second_inputs(seed + 1).items():
        if name != "x":
            out[name + "_2"] = value
    return out


def reference(
    x, p, rel_bias, hgrn_lb, ffn1_pre_g, ffn1_post_g, ffn1_w_gate, ffn1_w_up, ffn1_w_down,
    mix_pre_g, mix_post_g, w_in, kv_norm_g, kidx_norm_g, w_uk, w_uv, hgrn_norm_g, w_br_a,
    w_br_b, b_gate, w_out, ffn2_pre_g, ffn2_post_g, ffn2_w_gate, ffn2_w_up, ffn2_w_down,
    ple_pre_g, ple_post_g, w_ple_gate, w_ple_proj, p_2, positions_2, rel_bias_table_2,
    attn_norm_2, a_w_qkv_2, a_q_norm_2, a_k_norm_2, a_lam_q1_2, a_lam_k1_2, a_lam_q2_2,
    a_lam_k2_2, a_sub_norm_2, a_w_o_2, kv_norm_2, w_dkv_2, ckv_norm_2, w_ukv_2, k_nope_norm_2,
    k_pe_norm_2, b_w_dq_2, b_cq_norm_2, b_w_uq_2, b_q_nope_norm_2, b_q_pe_norm_2, b_w_o_2,
    ffn_norm_2, ffn_w_in_2, ffn_conv_w_2, ffn_conv_b_2, ffn_w_out_2, ple_norm_2, ple_w_proj_2,
    ple_w_gate_2,
):
    x = first_block(
        x, p, rel_bias, hgrn_lb, ffn1_pre_g, ffn1_post_g, ffn1_w_gate, ffn1_w_up, ffn1_w_down,
        mix_pre_g, mix_post_g, w_in, kv_norm_g, kidx_norm_g, w_uk, w_uv, hgrn_norm_g, w_br_a,
        w_br_b, b_gate, w_out, ffn2_pre_g, ffn2_post_g, ffn2_w_gate, ffn2_w_up, ffn2_w_down,
        ple_pre_g, ple_post_g, w_ple_gate, w_ple_proj,
    )
    return second_block(
        x, p_2, positions_2, rel_bias_table_2, attn_norm_2, a_w_qkv_2, a_q_norm_2, a_k_norm_2,
        a_lam_q1_2, a_lam_k1_2, a_lam_q2_2, a_lam_k2_2, a_sub_norm_2, a_w_o_2, kv_norm_2,
        w_dkv_2, ckv_norm_2, w_ukv_2, k_nope_norm_2, k_pe_norm_2, b_w_dq_2, b_cq_norm_2,
        b_w_uq_2, b_q_nope_norm_2, b_q_pe_norm_2, b_w_o_2, ffn_norm_2, ffn_w_in_2, ffn_conv_w_2,
        ffn_conv_b_2, ffn_w_out_2, ple_norm_2, ple_w_proj_2, ple_w_gate_2,
    )


_drawn_inputs = setup_inputs


def setup_inputs(seed=0):
    import zlib

    import numpy as np

    out = dict(_drawn_inputs(seed))
    spreads = {}
    factors = {'rel_bias': 3.484,
     'kv_norm_g': 3.183,
     'b_gate': 8.0,
     'ffn2_post_g': 3.53,
     'ple_pre_g': 4.658,
     'a_q_norm_2': 2.97,
     'a_k_norm_2': 2.817,
     'a_lam_q2_2': 4.08,
     'a_lam_k2_2': 8.0,
     'a_sub_norm_2': 2.758,
     'kv_norm_2': 8.0,
     'ckv_norm_2': 7.652,
     'k_nope_norm_2': 8.0,
     'k_pe_norm_2': 8.0,
     'b_cq_norm_2': 8.0,
     'b_q_nope_norm_2': 8.0,
     'b_q_pe_norm_2': 8.0,
     'ffn_conv_b_2': 5.044,
     'ple_norm_2': 8.0}
    for name, (base, spread) in spreads.items():
        noise = np.random.default_rng([zlib.crc32(name.encode()), seed]).standard_normal(out[name].shape)
        drawn = base * np.exp(spread * noise) if base else spread * noise
        out[name] = __import__('jax').numpy.asarray(drawn.astype(out[name].dtype))
    for name, factor in factors.items():
        out[name] = (out[name] * factor).astype(out[name].dtype)
    return out
```

```python
import math
from contextlib import ExitStack

import numpy as np

import concourse.bass as bass
from concourse import mybir

F32 = mybir.dt.float32
F32R = mybir.dt.float32r
BF16 = mybir.dt.bfloat16
I32 = mybir.dt.int32
U8 = mybir.dt.uint8
ALU = mybir.AluOpType
ACT = mybir.ActivationFunctionType
AX = mybir.AxisListType

P = 128
T = 512
NB = T // P
D = 1024
KD = D // P
F = 2816
KF = F // P
EPS = 1e-6
SLOT = 8 * P
RAW_SLOTS = 4
SPLIT_SLOTS = 2
NEG = -1e30
TAKEN = -3e38
TOPK = min(256, T // 4)
TRI = [P * b * (b + 1) // 2 for b in range(NB + 1)]
UPPER = [0, 512, 896, 1152, 1280]
CREDIT = 64
BUCKETS = 32
MAX_DIST = 128
HEADS = 8
LAM_INIT = 0.8 - 0.6 * math.exp(-0.3 * 0)
ATT_SCALE = 64 ** -0.5
IDX_SCALE = HEADS ** -0.5 * 64 ** -0.5
LEVELS = 7


def bucket_starts():
    n = np.arange(1, 4 * MAX_DIST).astype(np.float32)
    half = BUCKETS // 2
    large = half + (np.log(n / np.float32(half)) / np.float32(math.log(MAX_DIST / half))
                    * np.float32(BUCKETS - half)).astype(np.int32)
    b = np.where(n < half, n.astype(np.int32), np.minimum(large, BUCKETS - 1))
    return [0] + [int(n[np.argmax(b >= j)]) for j in range(1, BUCKETS)]


class Events:

    def __init__(self, totals, rounds, events):
        self.order = {n: list(keys) for n, keys in events.items()}
        self.base = {n: totals.get(n, CREDIT) for n in events}
        for n, keys in self.order.items():
            assert len(keys) <= CREDIT, n
            totals[n] = self.base[n] + rounds * len(keys)

    def at(self, name, key=0, i=0, back=0):
        keys = self.order[name]
        return i * len(keys) + (self.base[name] + keys.index(key) + 1 - back)

    def before(self, name, key=0, i=0):
        return self.at(name, key, i, len(self.order[name]))


class Slots:

    def __init__(self, stream, sizes, rounds):
        n = len(sizes)
        assert n % SPLIT_SLOTS == 0 and sizes[0] == sizes[1] == SLOT
        self.sizes, self.rounds, self.first = sizes, rounds, stream["next"]
        self.uses = [sum(1 for p in range(n) if p % RAW_SLOTS == r) for r in range(RAW_SLOTS)]
        self.landed_base = list(stream["landed"])
        self.distance = [n + RAW_SLOTS] * n
        for i in range(rounds):
            for pos in range(n):
                r, at = pos % RAW_SLOTS, self.first + i * n + pos
                self.distance[pos] = min(self.distance[pos], at - stream["user"][r])
                stream["user"][r] = at
        for r in range(RAW_SLOTS):
            stream["landed"][r] += rounds * self.uses[r]
        stream["next"] += rounds * n

    def norm(self, i, pos):
        n = len(self.sizes)
        return (i, pos) if pos < n else (i + 1, pos - n)

    def landed(self, i, pos):
        r = pos % RAW_SLOTS
        return i * (16 * self.uses[r]) + 16 * (self.landed_base[r] + pos // RAW_SLOTS + 1)

    def split(self, i, pos):
        return i * len(self.sizes) + (RAW_SLOTS + self.first + pos + 1)

    def raw_free(self, i, pos):
        return i * len(self.sizes) + (RAW_SLOTS + self.first + pos - self.distance[pos] + 1)

    def hi_ready(self, i, pos):
        return i * len(self.sizes) + (self.first + pos + 1)

    def used(self, i, pos):
        return i * len(self.sizes) + (SPLIT_SLOTS + self.first + pos + 1)

    def split_free(self, i, pos):
        return i * len(self.sizes) + (self.first + pos + 1)


SEMS = """passed slot_hi slot_split slot_used barrier
 square square_summed mean_square log_ms rstd scaled x_hi x_lo x_lo_dve
 product act_hi act_lo evacuated squared acc_zero acc_sum added
 resid_scaled resid_dve resid_pool
 conv0 conv1 conv2 silu
 norm_sq norm_sum norm_log norm_rstd norm_out
 rows_turned rows_out idx_dots idx_relu idx_score topk_max topk_replace topk_masked mask_made
 pair_weights q_lat q_lat_out logits probs_raw row_min row_recip probs probs_t probs_t_out pv pv_out
 value_proj y_hi y_lo
 hg_sig hg_f hg_k hg_log hg_cum hg_cumexp hg_q hg_qg hg_kexp hg_kdec hg_g hg_v hg_turn hg_turn_out
 hg_diff hg_decay hg_x hg_a hg_a_out hg_kv hg_state hg_o hg_const
 gate prod_a prod_b merged
 bias_step bias_sel bias_mm bias_out rope_step rope_rot""".split()
DMA_SEMS = "loaded stored kidx_copied bias_in bias_stored0 bias_stored1 tile_in0 tile_in1".split()


class Kernel:

    def __init__(self, nc, ctx, dram, V):
        self.nc, self.dram, self.V = nc, dram, V

        def sb(name, shape, dt=F32, scope=ctx):
            return scope.enter_context(nc.sbuf_tensor(name, shape, dt))

        def overlay(*groups):
            size = [sum(int(np.prod(shape[1:])) * {BF16: 2, U8: 1}.get(dt, 4) for _, shape, dt in g) for g in groups]
            widest = size.index(max(size))
            placed = {}
            for n in [n for n in range(len(groups)) if n != widest] + [widest]:
                with ExitStack() as scope:
                    placed[n] = tuple(sb(name, shape, dt, ctx if n == widest else scope) for name, shape, dt in groups[n])
            return [placed[n] for n in range(len(groups))]

        self.consts = sb("consts", [P, dram["consts"].shape[1]])
        self.maskc = sb("maskc", [P, 2 * P], BF16)
        self.vecs = sb("vecs", [P, dram["vecs"].shape[1]])
        c = self.consts
        self.ones, self.half_ones = c[:, 0:P], c[:, P:2 * P]
        self.ident, self.rot = c[:, 2 * P:3 * P], c[:, 3 * P:4 * P]
        self.eps = c[:, 4 * P:4 * P + 1]
        self.log_half = c[:, 4 * P + 1:4 * P + 2]
        self.inv_freq = c[:, 4 * P + 2:4 * P + 3]
        self.starts = c[:, 4 * P + 3:4 * P + 4]
        self.log_keep = c[:, 4 * P + 4:4 * P + 5]
        self.log_scale = c[:, 4 * P + 5:4 * P + 6]
        self.log_att_scale = c[:, 4 * P + 6:4 * P + 7]
        self.ident_b, self.causal_b = self.maskc[:, 0:P], self.maskc[:, P:2 * P]
        self.h = sb("h", [P, KD, T])
        self.raw = [sb(f"raw{r}", [P, SLOT]) for r in range(RAW_SLOTS)]
        self.w_hi = [sb(f"w_hi{r}", [P, SLOT], F32R) for r in range(SPLIT_SLOTS)]
        self.w_lo = [sb(f"w_lo{r}", [P, SLOT], F32R) for r in range(SPLIT_SLOTS)]
        self.sq = [sb(f"sq{r}", [P, T]) for r in range(2)]
        self.tmp = [sb(f"tmp{r}", [P, T]) for r in range(4)]
        self.acc, self.rs = sb("acc", [P, T]), sb("rs", [P, T])
        self.small = sb("small", [P, 64])
        self.neg_lam = sb("neg_lam", [P, 1])
        (self.xh, self.xl), (self.y_over_x,) = overlay([("xh", [P, KD, T], F32R), ("xl", [P, KD, T], F32R)],
                                                       [("y_over_x", [P, KD, T], F32)])
        R, B = F32R, BF16
        (
            (self.ah, self.al),
            (self.yah, self.yal, self.ybh, self.ybl, self.mh, self.ml, self.y_mix),
            (_, self.kidx, self.ckt, self.ckr, self.wuk, self.wuv, self.key_mask, self.qa, self.w_idx, self.kw,
             self.ckt_raw, self.qi, self.score, self.relu, self.top8),
            (_, self.wuks, self.wuvs, self.qas, self.ql, self.dsa_e, self.dsa_pt, self.dsa_bias, self.dsa_o),
            (_, self.hf, self.hk, self.hq, self.hqg, self.hgl, self.hlog, self.hcum, self.hecum, self.hvt, self.hvr,
             self.hkd, self.hkdr, self.hdiff, self.hx, self.hat, self.hstate, self.hmask, self.hvec),
            (self.ph, self.pl, self.ptok, self.pp, self.y_ple),
            (self.oh, self.ol, self.dq, self.dk, self.dvt, self.dvr, self.de, self.dw, self.dpt, self.dbias),
            (self.cqh, self.cql, self.ckh, self.ckl, self.cos, self.sin, self.kpe, self.qpe, self.mq, self.mk,
             self.mvt, self.mvr, self.me, self.mpt, self.lat),
            (self.bpos, self.bposi, self.brow, self.browi, self.bsel, self.bout, self.btab, self.bdiag, self.lamv,
             self.lams),
        ) = overlay(
            [("ah", [P, KF, T], R), ("al", [P, KF, T], R)],
            [("yah", [P, 4, T], R), ("yal", [P, 4, T], R), ("ybh", [P, 4, T], R), ("ybl", [P, 4, T], R),
             ("mh", [P, KD, T], R), ("ml", [P, KD, T], R), ("y_mix", [P, KD, T], F32)],
            [("_hole1", [P, 16 * T], F32),
             ("kidx", [P, T], F32), ("ckt", [P, T], F32), ("ckr", [P, NB, P], F32), ("wuk", [P, 4 * P], F32),
             ("wuv", [P, 4 * P], F32), ("key_mask", [P, TRI[4]], B), ("qa", [P, 4, T], F32),
             ("w_idx", [P, NB, HEADS], F32),
             ("kw", [P, T], F32), ("ckt_raw", [P, T], F32), ("qi", [P, 4, T], F32), ("score", [P, TRI[4]], F32),
             ("relu", [P, 2, T], F32), ("top8", [P, 3, 8], F32)],
            [("_hole3", [P, 16 * T + 2 * T + NB * P + 8 * P + TRI[4] // 2 + 4 * T + NB * HEADS], F32),
             ("wuks", [P, P], F32), ("wuvs", [P, P], F32), ("qas", [P, T], F32), ("ql", [P, 2, T], F32),
             ("dsa_e", [P, 3, T], F32), ("dsa_pt", [P, 2, NB, T], F32), ("dsa_bias", [P, 2, T], F32),
             ("dsa_o", [P, T], F32)],
            [("_hole4", [P, 16 * T], F32),
             ("hf", [P, T], F32), ("hk", [P, T], F32), ("hq", [P, T], F32), ("hqg", [P, T], F32),
             ("hgl", [P, T], F32), ("hlog", [P, T], F32), ("hcum", [P, T], F32), ("hecum", [P, T], F32),
             ("hvt", [P, T], F32), ("hvr", [P, NB, P], F32), ("hkd", [P, T], F32), ("hkdr", [P, NB, P], F32),
             ("hdiff", [P, 2, T], F32), ("hx", [P, 2, T], F32), ("hat", [P, T], F32),
             ("hstate", [P, 3, P], F32), ("hmask", [P, LEVELS * P], U8), ("hvec", [P, 16], F32)],
            [("ph", [P, 2, T], R), ("pl", [P, 2, T], R), ("ptok", [P, 2, T], F32), ("pp", [P, KD, T], F32),
             ("y_ple", [P, KD, T], F32)],
            [("oh", [P, HEADS, T], R), ("ol", [P, HEADS, T], R), ("dq", [P, 2, T], F32), ("dk", [P, 2, T], F32),
             ("dvt", [P, T], F32), ("dvr", [P, 2, NB, P], F32), ("de", [P, 4, T], F32), ("dw", [P, 2, T], F32),
             ("dpt", [P, 2, NB, T], F32), ("dbias", [P, 2, TRI[4]], F32)],
            [("cqh", [P, 4, T], R), ("cql", [P, 4, T], R), ("ckh", [P, 2, T], R), ("ckl", [P, 2, T], R),
             ("cos", [P, T], F32), ("sin", [P, T], F32), ("kpe", [P, T], F32), ("qpe", [P, T], F32),
             ("mq", [P, 2, T], F32), ("mk", [P, 2, T], F32), ("mvt", [P, T], F32), ("mvr", [P, 2, NB, P], F32),
             ("me", [P, 3, T], F32), ("mpt", [P, 2, NB, T], F32), ("lat", [P, 4, T], F32)],
            [("bpos", [P, T], F32), ("bposi", [P, T], I32), ("brow", [P, P], F32), ("browi", [P, P], I32),
             ("bsel", [P, 4, T], F32), ("bout", [P, 2, T], F32), ("btab", [P, 2, HEADS], F32),
             ("bdiag", [P, 32], F32), ("lamv", [P, 4, 64], F32), ("lams", [P, 8], F32)],
        )
        self.ps = ctx.enter_context(nc.psum_tensor("ps", [P, 8, T], F32))
        self.sem = {n: ctx.enter_context(nc.semaphore(n)) for n in SEMS}
        self.landed = [ctx.enter_context(nc.semaphore(f"landed{r}")) for r in range(RAW_SLOTS)]
        self.dma = {n: ctx.enter_context(nc.semaphore(n)) for n in DMA_SEMS}
        self.dma_total = {n: 16 * n.startswith("bias_stored") for n in DMA_SEMS}
        self.totals = {}
        self.stream = {"next": 0, "landed": [0] * RAW_SLOTS, "user": [r - RAW_SLOTS for r in range(RAW_SLOTS)]}
        self.n_groups = 0

    def events(self, rounds=1, **events):
        return Events(self.totals, rounds, events)

    def slots(self, sizes, rounds):
        return Slots(self.stream, sizes, rounds)

    def load(self, sp, w, i, pos, src):
        sp.wait_ge(self.sem["slot_split"], w.raw_free(i, pos))
        sp.dma_start(self.raw[pos % RAW_SLOTS][:, 0:w.sizes[pos]], src).then_inc(self.landed[pos % RAW_SLOTS], 16)

    def round_hi(self, dve, w, i, pos):
        i, pos = w.norm(i, pos)
        r, s, n = pos % RAW_SLOTS, pos % SPLIT_SLOTS, w.sizes[pos]
        dve.wait_ge(self.landed[r], w.landed(i, pos))
        dve.wait_ge(self.sem["slot_used"], w.split_free(i, pos))
        dve.tensor_copy(self.w_hi[s][:, 0:n], self.raw[r][:, 0:n]).then_inc(self.sem["slot_hi"], 1)

    def take_lo(self, pool, w, i, pos):
        i, pos = w.norm(i, pos)
        r, s, n = pos % RAW_SLOTS, pos % SPLIT_SLOTS, w.sizes[pos]
        pool.wait_ge(self.sem["slot_hi"], w.hi_ready(i, pos))
        pool.tensor_tensor(self.w_lo[s][:, 0:n], self.raw[r][:, 0:n], self.w_hi[s][:, 0:n].bitcast(F32),
                           ALU.subtract).then_inc(self.sem["slot_split"], 1)

    def mm3(self, pe, out, s, col, xh, xl, start, stop):
        wh, wl = self.w_hi[s][:, col:col + P], self.w_lo[s][:, col:col + P]
        pe.matmul(out, wh, xh, start=start, stop=False)
        pe.matmul(out, wh, xl, start=False, stop=False)
        return pe.matmul(out, wl, xh, start=False, stop=stop)

    def panel(self, pe, w, i, pos, out, xh, xl, k0=0, nk=8, col=0, first=True, last=True, done=True,
              ready=None):
        if col == 0:
            pe.wait_ge(self.sem["slot_split"], w.split(i, pos))
        for k in range(nk):
            if ready is not None and ready(k0 + k) is not None:
                pe.wait_ge(*ready(k0 + k))
            mm = self.mm3(pe, out, pos % SPLIT_SLOTS, col + k * P, xh[:, k0 + k, :], xl[:, k0 + k, :],
                          first and k == 0, last and k == nk - 1)
        if done:
            mm.then_inc(self.sem["slot_used"], 1)
        return mm

    def moved(self, name, n=1):
        self.dma_total[name] += 16 * n
        return self.dma_total[name]

    def carry(self, eng):
        eng.sem_inc(self.sem["passed"], 1)

    def barrier(self, eng):
        eng.drain().then_inc(self.sem["barrier"], 1)

    def meet(self, eng, n):
        if n:
            eng.wait_ge(self.sem["barrier"], 4 * n)


class Stage:
    ROUNDS = 1

    def __init__(self, k, after=None):
        self.k, self.w, self.after = k, None, after
        if after is None:
            k.n_groups += 1
        self.number = k.n_groups - 1
        self.plan()

    def plan(self):
        pass

    def last(self, name, key=0):
        return self.k.sem[name], self.e.at(name, key, self.ROUNDS - 1)

    def of_tile(self, name, t, keys):
        return self.k.sem[name], self.e.at(name, t % keys, t // keys)

    def x_ready(self, t):
        return self.after.x_made(t) if self.after is not None else None

    def sync(self, sp):
        pass

    def inputs(self, act):
        pass

    def tensor(self, pe):
        pass

    def scalar(self, act):
        pass

    def vector(self, dve):
        pass

    def gpsimd(self, pool):
        pass


class Setup(Stage):

    def plan(self):
        self.done = self.k.moved("loaded", 4)

    def sync(self, sp):
        k = self.k
        for dst, name in ((k.consts[:], "consts"), (k.maskc[:], "maskc"), (k.vecs[:], "vecs"),
                          (k.h[:].rearrange("p a t -> p (a t)"), "x")):
            sp.dma_start(dst, k.dram[name]).then_inc(k.dma["loaded"], 16)

    def tensor(self, pe):
        pe.wait_ge(self.k.dma["loaded"], self.done)

    scalar = vector = gpsimd = tensor


class PreNorm(Stage):

    def __init__(self, k, gain, mode="square", after=None, source=None):
        self.gain, self.mode = gain, mode
        self.source = source if source is not None else after
        super().__init__(k, after)

    def plan(self):
        n = range(KD)
        sums = {"square": dict(square=n, square_summed=n), "summed": dict(square_summed=[KD - 1]), "again": {}}
        rstd = {} if self.mode == "again" else dict(log_ms=[0], rstd=[0])
        self.e = self.k.events(scaled=n, x_hi=n, x_lo=range(1, KD, 2), x_lo_dve=range(0, KD, 2), **rstd,
                               **sums[self.mode])

    def x_made(self, t):
        return self.last("x_lo" if t % 2 else "x_lo_dve", t)

    def tensor(self, pe):
        k, e = self.k, self.e
        if self.mode == "square":
            for t in range(KD):
                pe.wait_ge(k.sem["square"], e.at("square", t))
                pe.matmul(k.ps[:, 7, :], k.ones, k.sq[t % 2][:], start=t == 0, stop=t == KD - 1
                          ).then_inc(k.sem["square_summed"], 1)
        elif self.mode == "summed":
            pe.wait_ge(*self.source.last("acc_sum", 3))
            pe.matmul(k.ps[:, 7, :], k.ones, k.acc[:], start=True, stop=True).then_inc(k.sem["square_summed"], 1)

    def scalar(self, act):
        k, e = self.k, self.e
        if self.mode != "again":
            act.preload_act_table_set("natural_log_exp_and_others")
        if self.mode == "square":
            for t in range(KD):
                if self.source is not None:
                    act.wait_ge(*self.source.h_made(t))
                if t >= 2:
                    act.wait_ge(k.sem["square_summed"], e.at("square_summed", t - 2))
                act.activation(k.sq[t % 2][:], k.h[:, t, :], ACT.Square).then_inc(k.sem["square"], 1)
        if self.mode != "again":
            act.wait_ge(k.sem["square_summed"], e.at("square_summed", KD - 1))
            act.activation(k.sq[0][:], k.ps[:, 7, :], ACT.Ln, bias=k.eps, scale=1.0 / D).then_inc(k.sem["log_ms"], 1)
            act.wait_ge(k.sem["log_ms"], e.at("log_ms"))
            act.activation(k.rs[:], k.sq[0][:], ACT.Exp, scale=-0.5).then_inc(k.sem["rstd"], 1)
        for t in range(KD):
            act.wait_ge(k.sem["scaled"], e.at("scaled", t))
            act.activation(k.xh[:, t, :], k.tmp[t % 4][:], ACT.Copy).then_inc(k.sem["x_hi"], 1)

    def low(self, eng, t):
        k, e = self.k, self.e
        eng.wait_ge(k.sem["x_hi"], e.at("x_hi", t))
        return eng.tensor_tensor(k.xl[:, t, :], k.tmp[t % 4][:], k.xh[:, t, :].bitcast(F32), ALU.subtract)

    def vector(self, dve):
        k, e = self.k, self.e
        if self.mode != "again":
            dve.wait_ge(k.sem["rstd"], e.at("rstd"))
        elif self.after is not None:
            dve.wait_ge(*self.after.last("x_lo", self.after.n - 1))
            dve.wait_ge(*self.after.last("norm_out", 3))
        for t in range(KD):
            if t >= 4:
                dve.wait_ge(*self.x_made(t - 4))
            dve.scalar_tensor_tensor(k.tmp[t % 4][:], k.h[:, t, :], k.vecs[:, self.gain + t:self.gain + t + 1],
                                     k.rs[:], ALU.mult, ALU.mult).then_inc(k.sem["scaled"], 1)
            if t % 2:
                self.low(dve, t - 1).then_inc(k.sem["x_lo_dve"], 1)

    def gpsimd(self, pool):
        for t in range(1, KD, 2):
            self.low(pool, t).then_inc(self.k.sem["x_lo"], 1)


class SwigluUp(Stage):
    ROUNDS = KF // 2

    def __init__(self, k, weights, after=None):
        self.weights = k.dram[weights]
        super().__init__(k, after)

    def plan(self):
        self.w = self.k.slots([SLOT] * 4, self.ROUNDS)
        self.e = self.k.events(self.ROUNDS, silu=[0, 1], product=[0, 1], act_hi=[0, 1], act_lo=[0, 1])

    def a_made(self, t):
        return self.of_tile("act_lo", t, 2)

    def bank_read(self, j):
        return self.last("product", j // 2)

    def sync(self, sp):
        with sp.Fori(0, self.ROUNDS) as i:
            for pos in range(4):
                self.k.load(sp, self.w, i, pos, self.weights[4 * i + pos])

    def tensor(self, pe):
        k, e = self.k, self.e
        with pe.Fori(0, self.ROUNDS) as i:
            for pos in range(4):
                name = "silu" if pos % 2 == 0 else "product"
                pe.wait_ge(k.sem[name], e.before(name, pos // 2, i))
                k.panel(pe, self.w, i, pos, k.ps[:, pos, :], k.xh, k.xl, ready=self.x_ready if pos == 0 else None)

    def scalar(self, act):
        k, e = self.k, self.e
        with act.Fori(0, self.ROUNDS) as i:
            for pair in range(2):
                act.wait_ge(k.sem["slot_used"], self.w.used(i, 2 * pair))
                act.wait_ge(k.sem["product"], e.before("product", pair, i))
                act.activation(k.sq[pair][:], k.ps[:, 2 * pair, :], ACT.Silu).then_inc(k.sem["silu"], 1)
                act.wait_ge(k.sem["product"], e.at("product", pair, i))
                act.activation(k.ah[:, 2 * i + pair, :], k.tmp[pair][:], ACT.Copy).then_inc(k.sem["act_hi"], 1)

    def vector(self, dve):
        k, e = self.k, self.e
        with dve.Fori(0, self.ROUNDS) as i:
            for pos in range(4):
                k.round_hi(dve, self.w, i, pos + 2)
                if pos % 2 == 1:
                    pair = pos // 2
                    dve.wait_ge(k.sem["slot_used"], self.w.used(i, pos))
                    dve.wait_ge(k.sem["silu"], e.at("silu", pair, i))
                    dve.wait_ge(k.sem["act_lo"], e.before("act_lo", pair, i))
                    dve.tensor_tensor(k.tmp[pair][:], k.ps[:, pos, :], k.sq[pair][:], ALU.mult
                                      ).then_inc(k.sem["product"], 1)

    def gpsimd(self, pool):
        k, e = self.k, self.e
        with pool.Fori(0, self.ROUNDS) as i:
            for pos in range(4):
                k.take_lo(pool, self.w, i, pos + 2)
                if pos % 2 == 1:
                    pair = pos // 2
                    pool.wait_ge(k.sem["act_hi"], e.at("act_hi", pair, i))
                    pool.tensor_tensor(k.al[:, 2 * i + pair, :], k.tmp[pair][:],
                                       k.ah[:, 2 * i + pair, :].bitcast(F32), ALU.subtract
                                       ).then_inc(k.sem["act_lo"], 1)


class OutProj(Stage):
    ROUNDS = 2

    def __init__(self, k, weights, xh, xl, nk, into=None, summed=True, after=None):
        self.weights, self.xh, self.xl, self.nk, self.into = k.dram[weights], xh, xl, nk, into
        self.summed = summed
        super().__init__(k, after)

    def plan(self):
        n = -(-self.nk // 8)
        self.parts = [8] * (n - 1) + [self.nk - 8 * (n - 1)]
        self.down = self
        self.w = self.k.slots([p * P for p in self.parts] * 4, self.ROUNDS)
        n = range(4)
        names = dict(added=n) if self.into is None else dict(evacuated=n)
        if self.summed:
            names.update(squared=n, acc_sum=n)
        self.e = self.k.events(self.ROUNDS, **names)
        if self.summed:
            self.zero = self.k.events(1, acc_zero=[0])

    def sync(self, sp):
        with sp.Fori(0, self.ROUNDS) as i:
            for j in range(4):
                at = 0
                for q, part in enumerate(self.parts):
                    self.k.load(sp, self.w, i, j * len(self.parts) + q, self.weights[4 * i + j, :, at:at + part * P])
                    at += part * P

    def tensor(self, pe):
        k, e = self.k, self.e
        free = "squared" if self.into is not None else "added"
        with pe.Fori(0, self.ROUNDS) as i:
            for j in range(4):
                pe.wait_ge(k.sem[free], e.before(free, j, i))
                if self.after is not None:
                    pe.wait_ge(*self.after.bank_read(j))
                at = 0
                for q, part in enumerate(self.parts):
                    k.panel(pe, self.w, i, j * len(self.parts) + q, k.ps[:, j, :], self.xh, self.xl, at, part,
                            first=q == 0, last=q == len(self.parts) - 1,
                            ready=self.after.a_made if self.after is not None and j == 0 else None)
                    at += part

    def last_pos(self, j):
        return (j + 1) * len(self.parts) - 1

    def scalar(self, act):
        if not self.summed:
            return
        k, e = self.k, self.e
        with act.Fori(0, self.ROUNDS) as i:
            for j in range(4):
                if self.into is not None:
                    act.wait_ge(k.sem["slot_used"], self.w.used(i, self.last_pos(j)))
                    act.activation(self.into[:, 4 * i + j, :], k.ps[:, j, :], ACT.Copy).then_inc(k.sem["evacuated"], 1)
                    source = k.ps[:, j, :]
                else:
                    act.wait_ge(k.sem["added"], e.at("added", j, i))
                    source = k.h[:, 4 * i + j, :]
                before = e.at("acc_sum", j - 2, i) if j >= 2 else e.before("acc_sum", j + 2, i)
                act.wait_ge(k.sem["acc_sum"], before)
                act.activation(k.sq[j % 2][:], source, ACT.Square).then_inc(k.sem["squared"], 1)

    def vector(self, dve):
        k, e = self.k, self.e
        if self.summed:
            dve.memset(k.acc[:], 0.0).then_inc(k.sem["acc_zero"], 1)
            dve.wait_ge(k.sem["acc_zero"], self.zero.at("acc_zero"))
        with dve.Fori(0, self.ROUNDS) as i:
            for j in range(4):
                for q in range(len(self.parts)):
                    k.round_hi(dve, self.w, i, j * len(self.parts) + q + 2)
                if self.into is None:
                    dve.wait_ge(k.sem["slot_used"], self.w.used(i, self.last_pos(j)))
                    dve.tensor_tensor(k.h[:, 4 * i + j, :], k.ps[:, j, :], k.h[:, 4 * i + j, :], ALU.add
                                      ).then_inc(k.sem["added"], 1)
                if self.summed:
                    dve.wait_ge(k.sem["squared"], e.at("squared", j, i))
                    dve.wait_ge(k.sem["acc_sum"], e.at("acc_sum", j - 1, i) if j else e.before("acc_sum", 3, i))
                    dve.tensor_tensor(k.acc[:], k.acc[:], k.sq[j % 2][:], ALU.add).then_inc(k.sem["acc_sum"], 1)

    def gpsimd(self, pool):
        with pool.Fori(0, self.ROUNDS) as i:
            for pos in range(4 * len(self.parts)):
                self.k.take_lo(pool, self.w, i, pos + 2)


class Residual(Stage):

    def __init__(self, k, y, gain, halved, after):
        self.y, self.gain, self.halved = y, gain, halved
        super().__init__(k, after)

    def h_made(self, t):
        return self.last("resid_pool" if t % 2 else "resid_dve", t)

    def plan(self):
        self.down = self.after
        self.e = self.k.events(mean_square=[0], log_ms=[0], rstd=[0], resid_scaled=range(KD),
                               resid_dve=range(0, KD, 2), resid_pool=range(1, KD, 2))

    def tensor(self, pe):
        k = self.k
        pe.wait_ge(*self.after.last("acc_sum", 3))
        pe.matmul(k.ps[:, 7, :], k.ones, k.acc[:], start=True, stop=True).then_inc(k.sem["mean_square"], 1)

    def scalar(self, act):
        k, e = self.k, self.e
        act.preload_act_table_set("natural_log_exp_and_others")
        act.wait_ge(k.sem["mean_square"], e.at("mean_square"))
        act.activation(k.sq[0][:], k.ps[:, 7, :], ACT.Ln, bias=k.eps, scale=1.0 / D).then_inc(k.sem["log_ms"], 1)
        act.wait_ge(k.sem["log_ms"], e.at("log_ms"))
        extra = dict(bias=k.log_half) if self.halved else {}
        act.activation(k.rs[:], k.sq[0][:], ACT.Exp, scale=-0.5, **extra).then_inc(k.sem["rstd"], 1)

    def vector(self, dve):
        k, e = self.k, self.e
        dve.wait_ge(k.sem["rstd"], e.at("rstd"))
        for t in range(KD):
            if t >= 4:
                n = "resid_dve" if t % 2 == 0 else "resid_pool"
                dve.wait_ge(k.sem[n], e.at(n, t - 4))
            dve.scalar_tensor_tensor(k.tmp[t % 4][:], self.y[:, t, :], k.vecs[:, self.gain + t:self.gain + t + 1],
                                     k.rs[:], ALU.mult, ALU.mult).then_inc(k.sem["resid_scaled"], 1)
            if t % 2 == 0:
                dve.wait_ge(k.sem["resid_scaled"], e.at("resid_scaled", t))
                dve.tensor_tensor(k.h[:, t, :], k.tmp[t % 4][:], k.h[:, t, :], ALU.add
                                  ).then_inc(k.sem["resid_dve"], 1)

    def gpsimd(self, pool):
        k, e = self.k, self.e
        for t in range(1, KD, 2):
            pool.wait_ge(k.sem["resid_scaled"], e.at("resid_scaled", t))
            pool.tensor_tensor(k.h[:, t, :], k.tmp[t % 4][:], k.h[:, t, :], ALU.add).then_inc(k.sem["resid_pool"], 1)

class ConvUp(Stage):
    ROUNDS = KF // 2

    def __init__(self, k, weights, conv, after=None):
        self.weights, self.conv = k.dram[weights], conv
        super().__init__(k, after)

    def plan(self):
        self.w = self.k.slots([SLOT] * 4, self.ROUNDS)
        self.e = self.k.events(self.ROUNDS, conv0=range(4), conv1=range(4), conv2=range(4), silu=[0, 1],
                               product=[0, 1], act_hi=[0, 1], act_lo=[0, 1])

    sync, a_made = SwigluUp.sync, SwigluUp.a_made

    def bank_read(self, j):
        return self.last("conv2", j)

    def col(self, i, pos, c):
        at = i * 16 + (self.conv + 4 * pos + c)
        return self.k.vecs[:, bass.ds(at, 1)]

    def tensor(self, pe):
        k, e = self.k, self.e
        with pe.Fori(0, self.ROUNDS) as i:
            for pos in range(4):
                pe.wait_ge(k.sem["conv2"], e.before("conv2", pos, i))
                k.panel(pe, self.w, i, pos, k.ps[:, pos, :], k.xh, k.xl, ready=self.x_ready if pos == 0 else None)

    def scalar(self, act):
        k, e = self.k, self.e
        with act.Fori(0, self.ROUNDS) as i:
            for pair in range(2):
                for pos in (2 * pair, 2 * pair + 1):
                    act.wait_ge(k.sem["slot_used"], self.w.used(i, pos))
                    if pos % 2 == 0:
                        act.wait_ge(k.sem["act_lo"], e.before("act_lo", pair, i))
                    act.activation(k.tmp[pos][:], k.ps[:, pos, :], ACT.Identity, bias=self.col(i, pos, 3),
                                   scale=self.col(i, pos, 2)).then_inc(k.sem["conv0"], 1)
                act.wait_ge(k.sem["conv2"], e.at("conv2", 2 * pair + 1, i))
                act.activation(k.sq[pair][:], k.tmp[2 * pair + 1][:], ACT.Silu).then_inc(k.sem["silu"], 1)
                act.wait_ge(k.sem["product"], e.at("product", pair, i))
                act.activation(k.ah[:, 2 * i + pair, :], k.tmp[2 * pair][:], ACT.Copy).then_inc(k.sem["act_hi"], 1)

    def vector(self, dve):
        k, e = self.k, self.e
        with dve.Fori(0, self.ROUNDS) as i:
            for pos in range(4):
                k.round_hi(dve, self.w, i, pos + 2)
                for back, name, prev in ((1, "conv1", "conv0"), (2, "conv2", "conv1")):
                    dve.wait_ge(k.sem[prev], e.at(prev, pos, i))
                    dve.scalar_tensor_tensor(k.tmp[pos][:, back:T], k.ps[:, pos, 0:T - back], self.col(i, pos, 2 - back),
                                             k.tmp[pos][:, back:T], ALU.mult, ALU.add).then_inc(k.sem[name], 1)
                if pos % 2 == 1:
                    pair = pos // 2
                    dve.wait_ge(k.sem["silu"], e.at("silu", pair, i))
                    dve.tensor_tensor(k.tmp[2 * pair][:], k.tmp[2 * pair][:], k.sq[pair][:], ALU.mult
                                      ).then_inc(k.sem["product"], 1)

    def gpsimd(self, pool):
        k, e = self.k, self.e
        with pool.Fori(0, self.ROUNDS) as i:
            for pos in range(4):
                k.take_lo(pool, self.w, i, pos + 2)
                if pos % 2 == 1:
                    pair = pos // 2
                    pool.wait_ge(k.sem["act_hi"], e.at("act_hi", pair, i))
                    pool.tensor_tensor(k.al[:, 2 * i + pair, :], k.tmp[2 * pair][:],
                                       k.ah[:, 2 * i + pair, :].bitcast(F32), ALU.subtract
                                       ).then_inc(k.sem["act_lo"], 1)


class PleSplit(Stage):

    def __init__(self, k, tokens, after):
        self.tokens = k.dram[tokens]
        super().__init__(k, after)

    def plan(self):
        self.done = self.k.moved("loaded")
        self.e = self.k.events(1, act_hi=[0], act_lo=[0])

    def inputs(self, act):
        k = self.k
        act.wait_ge(k.sem["slot_used"], self.after.down.w.used(OutProj.ROUNDS - 1, len(self.after.down.w.sizes) - 1))
        act.dma_start(k.ptok[:].rearrange("p a t -> p (a t)"), self.tokens).then_inc(k.dma["loaded"], 16)

    def scalar(self, act):
        k = self.k
        act.wait_ge(k.dma["loaded"], self.done)
        act.activation(k.ph[:], k.ptok[:], ACT.Copy).then_inc(k.sem["act_hi"], 1)

    def gpsimd(self, pool):
        k, e = self.k, self.e
        pool.wait_ge(k.sem["act_hi"], e.at("act_hi"))
        pool.tensor_tensor(k.pl[:], k.ptok[:], k.ph[:].bitcast(F32), ALU.subtract).then_inc(k.sem["act_lo"], 1)


class PleProj(Stage):

    def __init__(self, k, weights, norm, split):
        self.weights, self.norm, self.split = k.dram[weights], norm, split
        super().__init__(k, norm)

    def plan(self):
        self.w = self.k.slots([SLOT] * 2, 1)
        self.e = self.k.events(1, evacuated=range(KD), product=range(KD))

    def x_made(self, t):
        return self.norm.x_made(t)

    def sync(self, sp):
        k = self.k
        for pos in range(2):
            k.load(sp, self.w, 0, pos, self.weights[pos])

    def tensor(self, pe):
        k, e = self.k, self.e
        pe.wait_ge(*self.split.last("act_lo"))
        for m in range(KD):
            pos = m // 4
            if m % 4 == 0:
                pe.wait_ge(k.sem["slot_split"], self.w.split(0, pos))
            if m == KD - 1:
                pe.wait_ge(*self.norm.last("log_ms"))
            for t in range(2):
                mm = k.mm3(pe, k.ps[:, m, :], pos % 2, (m % 4) * 2 * P + t * P, k.ph[:, t, :], k.pl[:, t, :],
                           t == 0, t == 1)
            mm.then_inc(k.sem["product"], 1)
            if m % 4 == 3:
                pe.wait_ge(k.sem["product"], e.at("product", m))
                pe.sem_inc(k.sem["slot_used"], 1)

    def scalar(self, act):
        k, e = self.k, self.e
        for m in range(KD):
            act.wait_ge(k.sem["product"], e.at("product", m))
            act.activation(k.pp[:, m, :], k.ps[:, m, :], ACT.Copy).then_inc(k.sem["evacuated"], 1)

    def vector(self, dve):
        for pos in range(2):
            self.k.round_hi(dve, self.w, 0, pos + 2)

    def gpsimd(self, pool):
        for pos in range(2):
            self.k.take_lo(pool, self.w, 0, pos + 2)


class PleGate(Stage):
    ROUNDS = 2

    def __init__(self, k, weights, normed, summed, after):
        self.weights, self.normed, self.summed = k.dram[weights], normed, summed
        super().__init__(k, after)

    def plan(self):
        self.w = self.k.slots([SLOT] * 4, self.ROUNDS)
        n = range(4)
        more = {} if self.normed else dict(added=n)
        if self.summed:
            more.update(squared=n, acc_sum=n)
        self.e = self.k.events(self.ROUNDS, gate=n, product=n, **more)
        if self.summed:
            self.zero = self.k.events(1, acc_zero=[0])

    def sync(self, sp):
        with sp.Fori(0, self.ROUNDS) as i:
            for pos in range(4):
                self.k.load(sp, self.w, i, pos, self.weights[4 * i + pos])

    def tensor(self, pe):
        k, e = self.k, self.e
        with pe.Fori(0, self.ROUNDS) as i:
            for pos in range(4):
                pe.wait_ge(k.sem["gate"], e.before("gate", pos, i))
                pe.wait_ge(*self.after.last("evacuated", pos))
                k.panel(pe, self.w, i, pos, k.ps[:, pos, :], k.xh, k.xl, ready=self.x_ready if pos == 0 else None)

    def scalar(self, act):
        k, e = self.k, self.e
        with act.Fori(0, self.ROUNDS) as i:
            for j in range(4):
                act.wait_ge(k.sem["slot_used"], self.w.used(i, j))
                act.wait_ge(k.sem["product"], e.at("product", j, i, back=2))
                act.activation(k.sq[j % 2][:], k.ps[:, j, :], ACT.Sigmoid).then_inc(k.sem["gate"], 1)
                if self.summed:
                    made, source = ("product", k.y_ple) if self.normed else ("added", k.h)
                    act.wait_ge(k.sem[made], e.at(made, j, i))
                    act.wait_ge(k.sem["acc_sum"], e.before("acc_sum", j, i))
                    act.activation(k.tmp[j][:], source[:, 4 * i + j, :], ACT.Square).then_inc(k.sem["squared"], 1)

    def vector(self, dve):
        k, e = self.k, self.e
        if self.summed:
            dve.memset(k.acc[:], 0.0).then_inc(k.sem["acc_zero"], 1)
            dve.wait_ge(k.sem["acc_zero"], self.zero.at("acc_zero"))
        with dve.Fori(0, self.ROUNDS) as i:
            for j in range(4):
                k.round_hi(dve, self.w, i, j + 2)
                dve.wait_ge(k.sem["gate"], e.at("gate", j, i))
                if self.normed:
                    dve.tensor_tensor(k.y_ple[:, 4 * i + j, :], k.sq[j % 2][:], k.pp[:, 4 * i + j, :], ALU.mult
                                      ).then_inc(k.sem["product"], 1)
                else:
                    if self.summed:
                        dve.wait_ge(k.sem["acc_sum"], e.before("acc_sum", j, i))
                    else:
                        dve.wait_ge(k.sem["added"], e.before("added", j, i))
                    dve.tensor_tensor(k.tmp[j][:], k.sq[j % 2][:], k.pp[:, 4 * i + j, :], ALU.mult
                                      ).then_inc(k.sem["product"], 1)
                    dve.wait_ge(k.sem["product"], e.at("product", j, i))
                    dve.tensor_tensor(k.h[:, 4 * i + j, :], k.tmp[j][:], k.h[:, 4 * i + j, :], ALU.add
                                      ).then_inc(k.sem["added"], 1)
                if self.summed:
                    dve.wait_ge(k.sem["squared"], e.at("squared", j, i))
                    dve.wait_ge(k.sem["acc_sum"], e.at("acc_sum", j, i, back=1))
                    dve.tensor_tensor(k.acc[:], k.acc[:], k.tmp[j][:], ALU.add).then_inc(k.sem["acc_sum"], 1)

    def gpsimd(self, pool):
        with pool.Fori(0, self.ROUNDS) as i:
            for pos in range(4):
                self.k.take_lo(pool, self.w, i, pos + 2)


class MixProj(Stage):
    COUNT = 10

    def plan(self):
        self.weights = self.k.dram["mix_first"]
        self.w = self.k.slots([SLOT] * self.COUNT, 1)
        self.e = self.k.events(1, evacuated=range(self.COUNT), norm_sq=[0, 1], norm_sum=[0, 1], norm_log=[0, 1],
                               norm_rstd=[0, 1], norm_out=[0, 1], rows_turned=[0, 1], rows_out=[0, 1])
        self.copied = self.k.moved("kidx_copied")
        self.done = self.k.moved("loaded", 2)

    def sync(self, sp):
        k = self.k
        for pos in range(self.COUNT):
            k.load(sp, self.w, 0, pos, self.weights[pos])

    def inputs(self, act):
        k = self.k
        act.dma_start(k.wuk[:], k.dram["w_uk"]).then_inc(k.dma["loaded"], 16)
        act.dma_start(k.wuv[:], k.dram["w_uv"]).then_inc(k.dma["loaded"], 16)

    def tensor(self, pe):
        k, e = self.k, self.e

        def norm_sum(n, rows):
            if n:
                pe.wait_ge(k.sem["norm_log"], e.at("norm_log", n - 1))
            pe.wait_ge(k.sem["norm_sq"], e.at("norm_sq", n))
            pe.matmul(k.ps[0:rows, 7, :], k.ones[0:rows, 0:rows], k.sq[n][0:rows, :], start=True, stop=True
                      ).then_inc(k.sem["norm_sum"], 1)

        for pos in range(self.COUNT):
            if pos >= 6:
                pe.wait_ge(k.sem["evacuated"], e.at("evacuated", pos - 6))
            k.panel(pe, self.w, 0, pos, k.ps[:, pos % 6, :], k.xh, k.xl, ready=self.x_ready if pos == 0 else None)
            if pos == 1:
                norm_sum(0, 64)
            if pos == 2:
                norm_sum(1, P)
            if pos == 5:
                pe.wait_ge(k.sem["norm_out"], e.at("norm_out", 1))
                for b in range(NB):
                    mm = pe.transpose(k.ps[:, 6, b * P:(b + 1) * P], k.ckt[:, b * P:(b + 1) * P], k.ident)
                mm.then_inc(k.sem["rows_turned"], 1)
                pe.wait_ge(k.sem["norm_log"], e.at("norm_log", 1))
                for b in range(NB):
                    mm = pe.transpose(k.ps[:, 7, b * HEADS:(b + 1) * HEADS], k.kw[64:64 + HEADS, b * P:(b + 1) * P],
                                      k.ident[64:64 + HEADS, 64:64 + HEADS])
                mm.then_inc(k.sem["rows_turned"], 1)

    def scalar(self, act):
        k, e = self.k, self.e
        act.preload_act_table_set("natural_log_exp_and_others")
        into = [k.kw[:], k.ckt_raw[:]] + [k.qi[:, n, :] for n in range(4)] + [k.qa[:, n, :] for n in range(4)]

        def evacuate(pos):
            act.wait_ge(k.sem["slot_used"], self.w.used(0, pos))
            act.activation(into[pos], k.ps[:, pos % 6, :], ACT.Copy).then_inc(k.sem["evacuated"], 1)

        def norm(n, rows):
            act.wait_ge(k.sem["norm_sum"], e.at("norm_sum", n))
            act.activation(k.tmp[n][0:rows, :], k.ps[0:rows, 7, :], ACT.Ln, bias=k.eps[0:rows, :], scale=1.0 / rows
                           ).then_inc(k.sem["norm_log"], 1)
            act.wait_ge(k.sem["norm_log"], e.at("norm_log", n))
            act.activation(k.tmp[2 + n][0:rows, :], k.tmp[n][0:rows, :], ACT.Exp, scale=-0.5
                           ).then_inc(k.sem["norm_rstd"], 1)

        for n, rows in ((0, 64), (1, P)):
            evacuate(n)
            act.wait_ge(k.sem["evacuated"], e.at("evacuated", n))
            act.activation(k.sq[n][0:rows, :], into[n][0:rows, :], ACT.Square).then_inc(k.sem["norm_sq"], 1)
        norm(0, 64)
        evacuate(2)
        norm(1, P)
        for pos in range(3, 6):
            evacuate(pos)
        act.wait_ge(k.sem["norm_out"], e.at("norm_out", 0))
        act.dma_start(k.kidx[64:P, :], k.kidx[0:64, :]).then_inc(k.dma["kidx_copied"], 16)
        act.wait_ge(k.sem["rows_turned"], e.at("rows_turned", 0))
        act.activation(k.ckr[:].rearrange("p b c -> p (b c)"), k.ps[:, 6, :], ACT.Copy).then_inc(k.sem["rows_out"], 1)
        act.wait_ge(k.sem["rows_turned"], e.at("rows_turned", 1))
        act.activation(k.w_idx[:].rearrange("p b c -> p (b c)"), k.ps[:, 7, 0:NB * HEADS], ACT.Copy, scale=IDX_SCALE
                       ).then_inc(k.sem["rows_out"], 1)
        for pos in range(6, self.COUNT):
            evacuate(pos)
        act.wait_ge(k.dma["kidx_copied"], self.copied)
        act.wait_ge(k.dma["loaded"], self.done)

    def vector(self, dve):
        k, e = self.k, self.e
        for pos in range(self.COUNT):
            k.round_hi(dve, self.w, 0, pos + 2)
            if pos in (2, 3):
                n, rows, src, dst = ((0, 64, k.kw, k.kidx), (1, P, k.ckt_raw, k.ckt))[pos - 2]
                at = k.V["kidx_norm_g" if n == 0 else "kv_norm_g"]
                gain = k.vecs[0:rows, at:at + 1]
                dve.wait_ge(k.sem["norm_rstd"], e.at("norm_rstd", n))
                dve.scalar_tensor_tensor(dst[0:rows, :], src[0:rows, :], gain, k.tmp[2 + n][0:rows, :],
                                         ALU.mult, ALU.mult).then_inc(k.sem["norm_out"], 1)

    def gpsimd(self, pool):
        for pos in range(self.COUNT):
            self.k.take_lo(pool, self.w, 0, pos + 2)


class IdxScore(Stage):
    UNITS = [(h, b) for h in range(HEADS) for b in range(1, NB)]

    def plan(self):
        n = range(len(self.UNITS))
        self.e = self.k.events(1, idx_dots=n, idx_relu=n, idx_score=n)

    def tensor(self, pe):
        k, e = self.k, self.e
        for n, (h, b) in enumerate(self.UNITS):
            lo = 64 * (h % 2)
            if n >= 4:
                pe.wait_ge(k.sem["idx_relu"], e.at("idx_relu", n - 4))
            pe.matmul(k.ps[:, n % 4, 0:P * (b + 1)], k.qi[lo:lo + 64, h // 2, b * P:(b + 1) * P],
                      k.kidx[lo:lo + 64, 0:P * (b + 1)], start=True, stop=True).then_inc(k.sem["idx_dots"], 1)

    def scalar(self, act):
        k, e = self.k, self.e
        for n, (h, b) in enumerate(self.UNITS):
            act.wait_ge(k.sem["idx_dots"], e.at("idx_dots", n))
            if n >= 2:
                act.wait_ge(k.sem["idx_score"], e.at("idx_score", n - 2))
            act.activation(k.relu[:, n % 2, 0:P * (b + 1)], k.ps[:, n % 4, 0:P * (b + 1)], ACT.Relu
                           ).then_inc(k.sem["idx_relu"], 1)

    def vector(self, dve):
        k, e = self.k, self.e
        for n, (h, b) in enumerate(self.UNITS):
            dve.wait_ge(k.sem["idx_relu"], e.at("idx_relu", n))
            score = k.score[:, TRI[b]:TRI[b + 1]]
            relu, w = k.relu[:, n % 2, 0:P * (b + 1)], k.w_idx[:, b, h:h + 1]
            if h == 0:
                dve.tensor_scalar(score, relu, w, None, ALU.mult).then_inc(k.sem["idx_score"], 1)
            else:
                dve.wait_ge(k.sem["idx_score"], e.at("idx_score", n - 3))
                dve.scalar_tensor_tensor(score, relu, w, score, ALU.mult, ALU.add).then_inc(k.sem["idx_score"], 1)


class TopK(Stage):

    def plan(self):
        n = range(TOPK // 8 * 3)
        self.e = self.k.events(1, topk_masked=range(3), topk_max=n, topk_replace=n, mask_made=range(NB))

    def vector(self, dve):
        k, e = self.k, self.e
        part = [k.score[:, TRI[b]:TRI[b + 1]] for b in range(NB)]
        for b in range(1, NB):
            own = part[b][:, b * P:(b + 1) * P]
            dve.tensor_tensor(own, own, k.causal_b, ALU.add).then_inc(k.sem["topk_masked"], 1)
        dve.wait_ge(k.sem["topk_masked"], e.at("topk_masked", 2))
        for r in range(TOPK // 8):
            for b in range(1, NB):
                n = 3 * r + b - 1
                if r:
                    dve.wait_ge(k.sem["topk_replace"], e.at("topk_replace", n - 3))
                dve.max(k.top8[:, b - 1, :], part[b]).then_inc(k.sem["topk_max"], 1)
            for b in range(1, NB):
                n = 3 * r + b - 1
                dve.wait_ge(k.sem["topk_max"], e.at("topk_max", n))
                dve.match_replace(part[b], k.top8[:, b - 1, :], part[b], TAKEN).then_inc(k.sem["topk_replace"], 1)
        for b in range(NB):
            mask = k.key_mask[:, TRI[b]:TRI[b + 1]]
            if b == 0:
                dve.tensor_copy(mask, k.causal_b).then_inc(k.sem["mask_made"], 1)
            else:
                dve.wait_ge(k.sem["topk_replace"], e.at("topk_replace", TOPK // 8 * 3 - 4 + b))
                dve.tensor_scalar(mask, part[b], TAKEN / 2, NEG, ALU.is_gt, ALU.mult).then_inc(k.sem["mask_made"], 1)


class DsaHeads(Stage):
    ROUNDS = HEADS // 2

    def plan(self):
        u, two = range(8), range(2)
        self.e = self.k.events(self.ROUNDS, pair_weights=range(3), q_lat=two, q_lat_out=two, logits=u, row_min=u,
                               probs_raw=u, row_recip=u, probs=u, probs_t=u, probs_t_out=u, pv=two, pv_out=two,
                               value_proj=two, y_hi=two, y_lo=two)
        self.tile_base = [self.k.moved(f"tile_in{j}", self.ROUNDS) - 16 * self.ROUNDS for j in range(2)]

    def tensor(self, pe):
        k, e = self.k, self.e

        def transposes(n):
            j, b = n // 4, n % 4
            pe.wait_ge(k.sem["probs"], e.at("probs", n, i))
            pe.wait_ge(k.sem["probs_t_out"], e.at("probs_t_out", n, i, back=2))
            for s in range(b + 1):
                mm = pe.transpose(k.ps[:, 3 + n % 2, s * P:(s + 1) * P], k.dsa_e[:, n % 3, s * P:(s + 1) * P], k.ident)
            mm.then_inc(k.sem["probs_t"], 1)
            if b == 3:
                pe.wait_ge(k.sem["probs_t_out"], e.at("probs_t_out", n, i))
                pe.wait_ge(k.sem["pv_out"], e.before("pv_out", j, i))
                for s in range(NB):
                    mm = pe.matmul(k.ps[:, 5 + j, s * P:T], k.ckr[:, s, :], k.dsa_pt[:, j, s, s * P:T],
                                   start=s == 0, stop=s == NB - 1)
                mm.then_inc(k.sem["pv"], 1)
                pe.wait_ge(k.sem["pv_out"], e.at("pv_out", j, i))
                if j == 0:
                    pe.wait_ge(k.sem["q_lat_out"], e.at("q_lat_out", 1, i))
                else:
                    pe.wait_ge(k.sem["y_lo"], e.at("y_lo", 0, i))
                pe.matmul(k.ps[64 * j:64 * j + 64, 7, :], k.wuvs[:, 64 * j:64 * j + 64], k.dsa_o[:],
                          start=True, stop=True).then_inc(k.sem["value_proj"], 1)

        with pe.Fori(0, self.ROUNDS) as i:
            for j in range(2):
                pe.wait_ge(k.sem["pair_weights"], e.at("pair_weights", 2, i))
                if j == 0:
                    pe.wait_ge(k.sem["y_lo"], e.before("y_lo", 1, i))
                else:
                    pe.wait_ge(k.sem["q_lat_out"], e.at("q_lat_out", 0, i))
                pe.matmul(k.ps[:, 7, :], k.wuks[64 * j:64 * j + 64, :], k.qas[64 * j:64 * j + 64, :],
                          start=True, stop=True).then_inc(k.sem["q_lat"], 1)
            for n in range(8 + 2):
                if n < 8:
                    j, b = n // 4, n % 4
                    if b == 0:
                        pe.wait_ge(k.sem["q_lat_out"], e.at("q_lat_out", j, i))
                    pe.wait_ge(k.sem["row_min"], e.at("row_min", n, i, back=3))
                    out = k.ps[:, n % 3, 0:P * (b + 1)]
                    pe.matmul(out, k.ql[:, j, b * P:(b + 1) * P], k.ckt[:, 0:P * (b + 1)], start=True, stop=False)
                    pe.matmul(out, k.ident_b, k.key_mask[:, TRI[b]:TRI[b + 1]], start=False, stop=True
                              ).then_inc(k.sem["logits"], 1)
                if n >= 2:
                    transposes(n - 2)

    def scalar(self, act):
        k, e = self.k, self.e
        act.preload_act_table_set("natural_log_exp_and_others")

        def turned_out(n):
            j, b = n // 4, n % 4
            if b == 0:
                act.wait_ge(k.sem["pv"], e.before("pv", j, i))
            act.wait_ge(k.sem["probs_t"], e.at("probs_t", n, i))
            act.activation(k.dsa_pt[:, j, 0:b + 1, b * P:(b + 1) * P],
                           k.ps[:, 3 + n % 2, 0:P * (b + 1)].rearrange("p (s q) -> p s q", q=P), ACT.Copy
                           ).then_inc(k.sem["probs_t_out"], 1)
            if b == 3:
                act.wait_ge(k.sem["pv"], e.at("pv", j, i))
                act.wait_ge(k.sem["value_proj"], e.at("value_proj", j, i, back=1))
                act.activation(k.dsa_o[:], k.ps[:, 5 + j, :], ACT.Copy).then_inc(k.sem["pv_out"], 1)
                act.wait_ge(k.sem["value_proj"], e.at("value_proj", j, i))
                act.activation(k.yah[64 * j:64 * j + 64, i, :], k.ps[64 * j:64 * j + 64, 7, :], ACT.Copy
                               ).then_inc(k.sem["y_hi"], 1)

        strip = k.dram["strip"].rearrange("(q h) s -> h q s", h=HEADS)
        with act.Fori(0, self.ROUNDS) as i:
            for j in range(2):
                act.wait_ge(k.sem["row_min"], e.before("row_min", 4 * j + 3, i))
                act.dma_start(k.dsa_bias[:, j, :], strip[2 * i + j]).then_inc(k.dma[f"tile_in{j}"], 16)
            for j in range(2):
                act.wait_ge(k.sem["q_lat"], e.at("q_lat", j, i))
                act.activation(k.ql[:, j, :], k.ps[:, 7, :], ACT.Copy, scale=ATT_SCALE).then_inc(k.sem["q_lat_out"], 1)
            for n in range(8 + 2):
                if n < 8:
                    b = n % 4
                    tile = k.dsa_e[:, n % 3, 0:P * (b + 1)]
                    act.wait_ge(k.sem["row_min"], e.at("row_min", n, i))
                    act.activation(tile, tile, ACT.Exp, bias=k.small[:, n:n + 1], scale=-1.0,
                                   accum_out=k.small[:, 16 + n:17 + n]).then_inc(k.sem["probs_raw"], 1)
                if n >= 2:
                    turned_out(n - 2)

    def vector(self, dve):
        k, e = self.k, self.e

        def normalize(n):
            b = n % 4
            dve.wait_ge(k.sem["probs_raw"], e.at("probs_raw", n, i))
            dve.reciprocal(k.small[:, 32 + n:33 + n], k.small[:, 16 + n:17 + n]).then_inc(k.sem["row_recip"], 1)
            dve.wait_ge(k.sem["row_recip"], e.at("row_recip", n, i))
            tile = k.dsa_e[:, n % 3, 0:P * (b + 1)]
            dve.tensor_scalar(tile, tile, k.small[:, 32 + n:33 + n], None, ALU.mult).then_inc(k.sem["probs"], 1)

        def low(j):
            dve.wait_ge(k.sem["y_hi"], e.at("y_hi", j, i))
            dve.tensor_tensor(k.yal[64 * j:64 * j + 64, i, :], k.ps[64 * j:64 * j + 64, 7, :],
                              k.yah[64 * j:64 * j + 64, i, :].bitcast(F32), ALU.subtract).then_inc(k.sem["y_lo"], 1)

        with dve.Fori(0, self.ROUNDS) as i:
            dve.wait_ge(k.sem["q_lat"], e.before("q_lat", 1, i))
            dve.tensor_copy(k.wuks[:], k.wuk[:, bass.ds(i * P, P)]).then_inc(k.sem["pair_weights"], 1)
            dve.tensor_copy(k.qas[:], k.qa[:, i, :]).then_inc(k.sem["pair_weights"], 1)
            dve.wait_ge(k.sem["value_proj"], e.before("value_proj", 1, i))
            dve.tensor_copy(k.wuvs[:], k.wuv[:, bass.ds(i * P, P)]).then_inc(k.sem["pair_weights"], 1)
            for n in range(8 + 3):
                if n < 8:
                    j, b = n // 4, n % 4
                    if b == 0:
                        dve.wait_ge(k.dma[f"tile_in{j}"], i * 16 + (self.tile_base[j] + 16))
                    dve.wait_ge(k.sem["logits"], e.at("logits", n, i))
                    dve.wait_ge(k.sem["probs_t"], e.at("probs_t", n, i, back=3))
                    k.carry(dve)
                    dve.tensor_tensor_reduce(k.dsa_e[:, n % 3, 0:P * (b + 1)], k.ps[:, n % 3, 0:P * (b + 1)],
                                             k.dsa_bias[:, j, T - P * (b + 1):T], -1.0, 3e38, ALU.add, ALU.min,
                                             k.small[:, n:n + 1]).then_inc(k.sem["row_min"], 1)
                if 1 <= n < 9:
                    normalize(n - 1)
                if n == 6:
                    low(0)
            low(1)


class Hgrn(Stage):
    ROUNDS = 4
    F_, Q_, I_, G_ = range(4)

    def plan(self):
        self.weights = self.k.dram["hgrn"]
        self.w = self.k.slots([SLOT] * 4, self.ROUNDS)
        lv, pair = range(LEVELS + 1), range(2)
        self.c = self.k.events(1, hg_const=range(9))
        self.e = self.k.events(
            self.ROUNDS, hg_sig=[0], hg_f=[0], hg_k=[0], hg_log=[0], hg_cum=range(NB), hg_cumexp=[0], hg_q=[0],
            hg_qg=[0], hg_kexp=range(NB - 1), hg_kdec=[0], hg_g=[0], hg_v=[0], hg_turn=pair, hg_turn_out=pair,
            hg_diff=range(2 * LEVELS), hg_decay=range(1, LEVELS + 1), hg_x=range(2 * LEVELS), hg_a=lv, hg_a_out=lv,
            hg_kv=[0], hg_state=range(3), hg_o=[0], norm_sq=[0], norm_sum=[0], norm_log=[0], norm_rstd=[0],
            norm_out=pair, y_hi=[0], y_lo=[0])
        self.done = self.k.moved("loaded")
        self.level_masks = self.k.hdiff[:].rearrange("p a t -> p (a t)")[:, 0:LEVELS * P]

    def sync(self, sp):
        k = self.k
        with sp.Fori(0, self.ROUNDS) as i:
            for pos in range(4):
                k.load(sp, self.w, i, pos, self.weights[4 * i + pos])

    def inputs(self, act):
        act.dma_start(self.level_masks, self.k.dram["level_masks"]).then_inc(self.k.dma["loaded"], 16)

    def tensor(self, pe):
        k, e = self.k, self.e
        with pe.Fori(0, self.ROUNDS) as i:
            for pos, reader in enumerate(("hg_sig", "hg_q", "hg_v", "hg_g")):
                pe.wait_ge(k.sem[reader], e.before(reader, 0, i))
                k.panel(pe, self.w, i, pos, k.ps[:, pos, :], k.xh, k.xl)
            pe.wait_ge(k.sem["hg_v"], e.at("hg_v", 0, i))
            pe.wait_ge(k.sem["norm_out"], e.before("norm_out", 0, i))
            for c in range(NB):
                mm = pe.transpose(k.ps[:, 6, c * P:(c + 1) * P], k.hvt[:, c * P:(c + 1) * P], k.ident)
            mm.then_inc(k.sem["hg_turn"], 1)
            for l in range(LEVELS + 1):
                pe.wait_ge(k.sem["hg_a_out"], e.at("hg_a_out", l, i, back=2))
                if l == 0:
                    pe.wait_ge(k.sem["hg_k"], e.at("hg_k", 0, i))
                    pe.wait_ge(k.sem["hg_q"], e.at("hg_q", 0, i))
                    keys, queries = k.hk, k.hq
                else:
                    pe.wait_ge(k.sem["hg_x"], e.at("hg_x", 2 * l - 1, i))
                    keys = queries = k.hx[:, l % 2, :]
                for c in range(NB):
                    mm = pe.matmul(k.ps[:, 4 + l % 2, c * P:(c + 1) * P], keys[:, c * P:(c + 1) * P],
                                   queries[:, c * P:(c + 1) * P], start=True, stop=True)
                mm.then_inc(k.sem["hg_a"], 1)
            pe.wait_ge(k.sem["hg_turn_out"], e.at("hg_turn_out", 0, i))
            pe.wait_ge(k.sem["hg_kdec"], e.at("hg_kdec", 0, i))
            for c in range(NB - 1):
                mm = pe.transpose(k.ps[:, 6, c * P:(c + 1) * P], k.hkd[:, c * P:(c + 1) * P], k.ident)
            mm.then_inc(k.sem["hg_turn"], 1)
            pe.wait_ge(k.sem["hg_turn_out"], e.at("hg_turn_out", 1, i))
            pe.wait_ge(k.sem["norm_log"], e.before("norm_log", 0, i))
            for c in range(NB - 1):
                mm = pe.matmul(k.ps[:, 7, c * P:(c + 1) * P], k.hkdr[:, c, :], k.hvr[:, c, :], start=True, stop=True)
            mm.then_inc(k.sem["hg_kv"], 1)
            pe.wait_ge(k.sem["hg_a_out"], e.at("hg_a_out", LEVELS, i))
            pe.wait_ge(k.sem["hg_qg"], e.at("hg_qg", 0, i))
            for c in range(NB):
                own = k.ps[:, 6, c * P:(c + 1) * P]
                mm = pe.matmul(own, k.hvr[:, c, :], k.hat[:, c * P:(c + 1) * P], start=True, stop=c == 0)
                if c:
                    pe.wait_ge(k.sem["hg_state"], e.at("hg_state", c - 1, i))
                    mm = pe.matmul(own, k.hstate[:, c - 1, :], k.hqg[:, c * P:(c + 1) * P], start=False, stop=True)
            mm.then_inc(k.sem["hg_o"], 1)
            pe.wait_ge(k.sem["norm_sq"], e.at("norm_sq", 0, i))
            pe.matmul(k.ps[:, 7, :], k.ones, k.sq[0][:], start=True, stop=True).then_inc(k.sem["norm_sum"], 1)

    def scalar(self, act):
        k, e, c = self.k, self.e, self.c
        act.wait_ge(k.sem["hg_const"], c.at("hg_const", 2))
        act.activation(k.hvec[:, 8:16], k.hvec[:, 8:16], ACT.Exp).then_inc(k.sem["hg_const"], 1)
        with act.Fori(0, self.ROUNDS) as i:
            act.wait_ge(k.sem["slot_used"], self.w.used(i, self.F_))
            act.wait_ge(k.sem["hg_a"], e.before("hg_a", 0, i))
            act.activation(k.hf[:], k.ps[:, self.F_, :], ACT.Sigmoid).then_inc(k.sem["hg_sig"], 1)
            act.wait_ge(k.sem["slot_used"], self.w.used(i, self.Q_))
            act.activation(k.hq[:], k.ps[:, self.Q_, :], ACT.Silu).then_inc(k.sem["hg_q"], 1)
            act.wait_ge(k.sem["slot_used"], self.w.used(i, self.I_))
            act.activation(k.hvt[:], k.ps[:, self.I_, :], ACT.Copy).then_inc(k.sem["hg_v"], 1)
            act.wait_ge(k.sem["slot_used"], self.w.used(i, self.G_))
            act.wait_ge(k.sem["norm_out"], e.before("norm_out", 1, i))
            act.activation(k.hgl[:], k.ps[:, self.G_, :], ACT.Silu).then_inc(k.sem["hg_g"], 1)
            act.preload_act_table_set("natural_log_exp_and_others")
            act.wait_ge(k.sem["hg_f"], e.at("hg_f", 0, i))
            act.activation(k.hlog[:], k.hf[:], ACT.Ln).then_inc(k.sem["hg_log"], 1)
            act.wait_ge(k.sem["hg_turn"], e.at("hg_turn", 0, i))
            act.activation(k.hvr[:].rearrange("p c v -> p (c v)"), k.ps[:, 6, :], ACT.Copy
                           ).then_inc(k.sem["hg_turn_out"], 1)
            act.wait_ge(k.sem["hg_cum"], e.at("hg_cum", NB - 1, i))
            act.activation(k.hecum[:], k.hcum[:], ACT.Exp).then_inc(k.sem["hg_cumexp"], 1)
            for c in range(NB - 1):
                act.activation(k.hkd[:, c * P:(c + 1) * P], k.hcum[:, c * P:(c + 1) * P], ACT.Exp, scale=-1.0,
                               bias=k.hcum[:, (c + 1) * P - 1:(c + 1) * P]).then_inc(k.sem["hg_kexp"], 1)
            for l in range(1, LEVELS + 1):
                act.wait_ge(k.sem["hg_diff"], e.at("hg_diff", 2 * l - 1, i))
                act.activation(k.hdiff[:, l % 2, :], k.hdiff[:, l % 2, :], ACT.Exp).then_inc(k.sem["hg_decay"], 1)
            act.wait_ge(k.sem["hg_turn"], e.at("hg_turn", 1, i))
            act.activation(k.hkdr[:, 0:NB - 1, :].rearrange("p c v -> p (c v)"), k.ps[:, 6, 0:(NB - 1) * P], ACT.Copy
                           ).then_inc(k.sem["hg_turn_out"], 1)
            act.wait_ge(k.sem["hg_o"], e.at("hg_o", 0, i))
            act.activation(k.sq[0][:], k.ps[:, 6, :], ACT.Square).then_inc(k.sem["norm_sq"], 1)
            act.wait_ge(k.sem["norm_sum"], e.at("norm_sum", 0, i))
            act.activation(k.sq[1][:], k.ps[:, 7, :], ACT.Ln, bias=k.eps, scale=1.0 / P).then_inc(k.sem["norm_log"], 1)
            act.wait_ge(k.sem["norm_log"], e.at("norm_log", 0, i))
            act.activation(k.rs[:], k.sq[1][:], ACT.Exp, scale=-0.5).then_inc(k.sem["norm_rstd"], 1)
            act.wait_ge(k.sem["norm_out"], e.at("norm_out", 1, i))
            act.activation(k.ybh[:, i, :], k.tmp[1][:], ACT.Copy).then_inc(k.sem["y_hi"], 1)

    def vector(self, dve):
        k, e, c, V = self.k, self.e, self.c, self.k.V
        v = k.hvec

        def const(ins, key):
            ins.then_inc(k.sem["hg_const"], 1)
            dve.wait_ge(k.sem["hg_const"], c.at("hg_const", key))

        b0, b1 = k.vecs[:, V["hgrn_lb0"]:V["hgrn_lb0"] + 4], k.vecs[:, V["hgrn_lb1"]:V["hgrn_lb1"] + 4]
        const(dve.tensor_tensor(v[:, 0:4], b0, b1, ALU.max), 0)
        const(dve.tensor_tensor(v[:, 8:12], b0, v[:, 0:4], ALU.subtract), 1)
        dve.tensor_tensor(v[:, 12:16], b1, v[:, 0:4], ALU.subtract).then_inc(k.sem["hg_const"], 1)
        dve.wait_ge(k.sem["hg_const"], c.at("hg_const", 3))
        const(dve.tensor_tensor(v[:, 4:8], v[:, 8:12], v[:, 12:16], ALU.add), 4)
        const(dve.reciprocal(v[:, 12:16], v[:, 4:8]), 5)
        const(dve.tensor_tensor(v[:, 0:4], v[:, 8:12], v[:, 12:16], ALU.mult), 6)
        const(dve.tensor_scalar(v[:, 4:8], v[:, 0:4], -1.0, 1.0, ALU.mult, ALU.add), 7)
        dve.wait_ge(k.dma["loaded"], self.done)
        const(dve.tensor_copy(k.hmask[:], self.level_masks), 8)

        def halves(x, l):
            L = P >> l
            x = x.rearrange("p (n w l) -> p n w l", w=2, l=L)
            return x[:, :, 0, :], x[:, :, 1, :], T // (2 * L), L

        def diff(l):
            first, second, n, L = halves(k.hcum[:], l)
            to_first, to_second, _, _ = halves(k.hdiff[:, l % 2, :], l)
            ref = first[:, :, L - 1:L].to_broadcast([P, n, L])
            dve.wait_ge(k.sem["hg_x"], e.at("hg_x", 2 * l - 1, i, back=4))
            dve.tensor_tensor(to_first, ref, first, ALU.subtract).then_inc(k.sem["hg_diff"], 1)
            dve.tensor_tensor(to_second, second, ref, ALU.subtract).then_inc(k.sem["hg_diff"], 1)

        def product(l):
            decay_first, decay_second, _, _ = halves(k.hdiff[:, l % 2, :], l)
            x_first, x_second, _, _ = halves(k.hx[:, l % 2, :], l)
            keys, _, _, _ = halves(k.hk[:], l)
            _, queries, _, _ = halves(k.hq[:], l)
            dve.wait_ge(k.sem["hg_decay"], e.at("hg_decay", l, i))
            dve.wait_ge(k.sem["hg_a"], e.at("hg_a", l, i, back=2))
            dve.tensor_tensor(x_first, keys, decay_first, ALU.mult).then_inc(k.sem["hg_x"], 1)
            dve.tensor_tensor(x_second, queries, decay_second, ALU.mult).then_inc(k.sem["hg_x"], 1)

        chunks = dict(q=P)
        hat = k.hat[:].rearrange("p (c q) -> p c q", **chunks)

        def a_out(l):
            dve.wait_ge(k.sem["hg_a"], e.at("hg_a", l, i))
            a = k.ps[:, 4 + l % 2, :].rearrange("p (c q) -> p c q", **chunks)
            if l == 0:
                dve.wait_ge(k.sem["hg_o"], e.before("hg_o", 0, i))
                dve.tensor_tensor(hat, a, k.ident.unsqueeze(1).to_broadcast([P, NB, P]), ALU.mult
                                  ).then_inc(k.sem["hg_a_out"], 1)
            else:
                dve.wait_ge(k.sem["hg_a_out"], e.at("hg_a_out", l - 1, i))
                k.carry(dve)
                mask = k.hmask[:, (l - 1) * P:l * P].unsqueeze(1).to_broadcast([P, NB, P])
                dve.copy_predicated(hat, mask, a).then_inc(k.sem["hg_a_out"], 1)

        with dve.Fori(0, self.ROUNDS) as i:
            k.round_hi(dve, self.w, i, 2)
            k.round_hi(dve, self.w, i, 3)
            dve.wait_ge(k.sem["hg_sig"], e.at("hg_sig", 0, i))
            dve.tensor_scalar(k.hf[:], k.hf[:], v[:, bass.ds(i + 4, 1)], v[:, bass.ds(i, 1)], ALU.mult, ALU.add
                              ).then_inc(k.sem["hg_f"], 1)
            dve.wait_ge(k.sem["hg_f"], e.at("hg_f", 0, i))
            dve.tensor_scalar(k.hk[:], k.hf[:], -1.0, 1.0, ALU.mult, ALU.add).then_inc(k.sem["hg_k"], 1)
            k.round_hi(dve, self.w, i, 4)
            k.round_hi(dve, self.w, i, 5)
            dve.wait_ge(k.sem["hg_log"], e.at("hg_log", 0, i))
            dve.wait_ge(k.sem["hg_kv"], e.before("hg_kv", 0, i))
            for b in range(NB):
                dve.tensor_tensor_scan(k.hcum[:, b * P:(b + 1) * P], k.ones, k.hlog[:, b * P:(b + 1) * P], 0.0,
                                       ALU.mult, ALU.add).then_inc(k.sem["hg_cum"], 1)
            dve.wait_ge(k.sem["hg_cum"], e.at("hg_cum", NB - 1, i))
            diff(1)
            dve.wait_ge(k.sem["hg_cumexp"], e.at("hg_cumexp", 0, i))
            dve.wait_ge(k.sem["hg_q"], e.at("hg_q", 0, i))
            dve.tensor_tensor(k.hqg[:], k.hq[:], k.hecum[:], ALU.mult).then_inc(k.sem["hg_qg"], 1)
            dve.wait_ge(k.sem["hg_kexp"], e.at("hg_kexp", NB - 2, i))
            own = (NB - 1) * P
            dve.tensor_tensor(k.hkd[:, 0:own], k.hkd[:, 0:own], k.hk[:, 0:own], ALU.mult).then_inc(k.sem["hg_kdec"], 1)
            a_out(0)
            for l in range(1, LEVELS + 1):
                if l < LEVELS:
                    diff(l + 1)
                product(l)
                if l >= 2:
                    a_out(l - 1)
            a_out(LEVELS)
            dve.wait_ge(k.sem["hg_kv"], e.at("hg_kv", 0, i))
            for c_ in range(NB - 1):
                kv = k.ps[:, 7, c_ * P:(c_ + 1) * P]
                if c_ == 0:
                    dve.tensor_copy(k.hstate[:, 0, :], kv).then_inc(k.sem["hg_state"], 1)
                else:
                    dve.wait_ge(k.sem["hg_state"], e.at("hg_state", c_ - 1, i))
                    dve.scalar_tensor_tensor(k.hstate[:, c_, :], k.hstate[:, c_ - 1, :],
                                             k.hecum[:, (c_ + 1) * P - 1:(c_ + 1) * P], kv, ALU.mult, ALU.add
                                             ).then_inc(k.sem["hg_state"], 1)
            dve.wait_ge(k.sem["norm_rstd"], e.at("norm_rstd", 0, i))
            dve.scalar_tensor_tensor(k.tmp[0][:], k.ps[:, 6, :], k.vecs[:, V["hgrn_norm_g"]:V["hgrn_norm_g"] + 1],
                                     k.rs[:], ALU.mult, ALU.mult).then_inc(k.sem["norm_out"], 1)
            dve.wait_ge(k.sem["norm_out"], e.at("norm_out", 0, i))
            dve.wait_ge(k.sem["y_lo"], e.before("y_lo", 0, i))
            dve.wait_ge(k.sem["hg_g"], e.at("hg_g", 0, i))
            dve.tensor_tensor(k.tmp[1][:], k.tmp[0][:], k.hgl[:], ALU.mult).then_inc(k.sem["norm_out"], 1)

    def gpsimd(self, pool):
        k, e = self.k, self.e
        with pool.Fori(0, self.ROUNDS) as i:
            for pos in range(4):
                k.take_lo(pool, self.w, i, pos + 2)
            pool.wait_ge(k.sem["y_hi"], e.at("y_hi", 0, i))
            pool.tensor_tensor(k.ybl[:, i, :], k.tmp[1][:], k.ybh[:, i, :].bitcast(F32), ALU.subtract
                               ).then_inc(k.sem["y_lo"], 1)


class Merge(Stage):
    ROUNDS = KD // 2

    def plan(self):
        self.weights = self.k.dram["merge"]
        self.w = self.k.slots([SLOT] * 6, self.ROUNDS)
        two = range(2)
        self.e = self.k.events(self.ROUNDS, gate=range(4), prod_a=two, prod_b=two, merged=two, x_hi=two, x_lo=two)

    def a_made(self, t):
        return self.of_tile("x_lo", t, 2)

    def bank_read(self, j):
        return self.last("prod_b", 0)

    def sync(self, sp):
        with sp.Fori(0, self.ROUNDS) as i:
            for pos in range(6):
                self.k.load(sp, self.w, i, pos, self.weights[6 * i + pos])

    def tensor(self, pe):
        k, e = self.k, self.e
        with pe.Fori(0, self.ROUNDS) as i:
            for j in range(2):
                for g in range(2):
                    pe.wait_ge(k.sem["gate"], e.before("gate", 2 * j + g, i))
                    k.panel(pe, self.w, i, 3 * j + g, k.ps[:, 4 * j + g, :], k.xh, k.xl)
                pe.wait_ge(k.sem["prod_b"], e.before("prod_b", j, i))
                k.panel(pe, self.w, i, 3 * j + 2, k.ps[:, 4 * j + 2, :], k.yah, k.yal, nk=4, done=False)
                k.panel(pe, self.w, i, 3 * j + 2, k.ps[:, 4 * j + 3, :], k.ybh, k.ybl, nk=4, col=4 * P)

    def scalar(self, act):
        k, e, V = self.k, self.e, self.k.V
        with act.Fori(0, self.ROUNDS) as i:
            for j in range(2):
                for g, (prod, bias) in enumerate((("prod_a", V["b_gate"]), ("prod_b", V["b_gate"] + KD))):
                    act.wait_ge(k.sem["slot_used"], self.w.used(i, 3 * j + g))
                    act.wait_ge(k.sem[prod], e.at(prod, j, i, back=1))
                    act.activation(k.sq[g][:], k.ps[:, 4 * j + g, :], ACT.Sigmoid,
                                   bias=k.vecs[:, bass.ds(2 * i + (bias + j), 1)]).then_inc(k.sem["gate"], 1)
                act.wait_ge(k.sem["merged"], e.at("merged", j, i))
                act.activation(k.mh[:, 2 * i + j, :], k.tmp[2 + j][:], ACT.Copy).then_inc(k.sem["x_hi"], 1)

    def vector(self, dve):
        k, e = self.k, self.e
        with dve.Fori(0, self.ROUNDS) as i:
            for j in range(2):
                for pos in range(3 * j, 3 * j + 3):
                    k.round_hi(dve, self.w, i, pos + 2)
                dve.wait_ge(k.sem["slot_used"], self.w.used(i, 3 * j + 2))
                dve.wait_ge(k.sem["gate"], e.at("gate", 2 * j + 1, i))
                dve.wait_ge(k.sem["merged"], e.at("merged", j, i, back=1))
                dve.tensor_tensor(k.tmp[0][:], k.ps[:, 4 * j + 2, :], k.sq[0][:], ALU.mult).then_inc(k.sem["prod_a"], 1)
                dve.tensor_tensor(k.tmp[1][:], k.ps[:, 4 * j + 3, :], k.sq[1][:], ALU.mult).then_inc(k.sem["prod_b"], 1)
                dve.wait_ge(k.sem["prod_b"], e.at("prod_b", j, i))
                dve.wait_ge(k.sem["x_lo"], e.before("x_lo", j, i))
                dve.tensor_tensor(k.tmp[2 + j][:], k.tmp[0][:], k.tmp[1][:], ALU.add).then_inc(k.sem["merged"], 1)

    def gpsimd(self, pool):
        k, e = self.k, self.e
        with pool.Fori(0, self.ROUNDS) as i:
            for j in range(2):
                for pos in range(3 * j, 3 * j + 3):
                    k.take_lo(pool, self.w, i, pos + 2)
                pool.wait_ge(k.sem["x_hi"], e.at("x_hi", j, i))
                pool.tensor_tensor(k.ml[:, 2 * i + j, :], k.tmp[2 + j][:], k.mh[:, 2 * i + j, :].bitcast(F32),
                                   ALU.subtract).then_inc(k.sem["x_lo"], 1)


class BiasTable(Stage):

    def __init__(self, k, table, positions, out, blocks, base, lam):
        self.table, self.positions, self.out = k.dram[table], positions, k.dram[out]
        self.blocks, self.base, self.lam = blocks, base, lam
        super().__init__(k)

    def plan(self):
        k = self.k
        n = 4 if self.lam else 0
        self.s = k.events(1, bias_step=range(6 + 1 + n))
        self.done = k.moved("bias_in", 6 + (1 if self.lam else 0))
        self.e, self.stored = [], []
        for b in self.blocks:
            self.stored.append([k.moved(f"bias_stored{r}", 4) - 64 for r in range(2)])
            self.e.append(k.events(4, bias_sel=range(8), bias_mm=range(2), bias_out=range(2)))

    def inputs(self, act):
        k = self.k
        key_pos, row_pos = k.dram[self.positions], k.dram[self.positions + "_rows"]
        sem = k.dma["bias_in"]
        act.dma_start(k.bposi[:], key_pos.to_broadcast([P, T])).then_inc(sem, 16)
        for q in range(4):
            act.dma_start(k.browi[32 * q:32 * q + 32, :], row_pos[q:q + 1, :].to_broadcast([32, P])).then_inc(sem, 16)
        act.dma_start(k.btab[:].rearrange("p a h -> p (a h)"), self.table).then_inc(sem, 16)
        if self.lam:
            act.dma_start(k.lamv[:].rearrange("p a d -> p (a d)"), k.dram["lam"].to_broadcast([P, 256])
                         ).then_inc(sem, 16)

    def tensor(self, pe):
        k = self.k
        pe.wait_ge(k.sem["bias_step"], self.s.at("bias_step", 6))
        for e, b in zip(self.e, self.blocks):
            width = P * (b + 1)
            with pe.Fori(0, 4) as i:
                for r in range(2):
                    pe.wait_ge(k.sem["bias_out"], e.before("bias_out", r, i))
                    for g in range(4):
                        n = 4 * r + g
                        pe.wait_ge(k.sem["bias_sel"], e.at("bias_sel", n, i))
                        mm = pe.matmul(k.ps[32 * g:32 * g + 32, r, 0:width], k.bdiag[:], k.bsel[:, g, 0:width],
                                       start=True, stop=True)
                    mm.then_inc(k.sem["bias_mm"], 1)

    def scalar(self, act):
        k = self.k
        if self.lam:
            act.wait_ge(k.sem["bias_step"], self.s.at("bias_step", 8))
            act.activation(k.lams[:, 2:4], k.lams[:, 0:2], ACT.Exp).then_inc(k.sem["bias_step"], 1)
        for e, b, stored in zip(self.e, self.blocks, self.stored):
            width = P * (b + 1)
            with act.Fori(0, 4) as i:
                for r in range(2):
                    act.wait_ge(k.sem["bias_mm"], e.at("bias_mm", r, i))
                    act.wait_ge(k.dma[f"bias_stored{r}"], i * 16 + stored[r])
                    act.activation(k.bout[:, r, 0:width], k.ps[:, r, 0:width], ACT.Copy).then_inc(k.sem["bias_out"], 1)
                    act.wait_ge(k.sem["bias_out"], e.at("bias_out", r, i))
                    row = i * (2 * P) + ((b - self.base) * P * HEADS + r * P)
                    act.dma_start(self.out[bass.ds(row, P), 0:width], k.bout[:, r, 0:width]
                                  ).then_inc(k.dma[f"bias_stored{r}"], 16)
        for r in range(2):
            act.wait_ge(k.dma[f"bias_stored{r}"], self.stored[-1][r] + 64)

    def vector(self, dve):
        k, s = self.k, self.s

        def step(ins, key):
            ins.then_inc(k.sem["bias_step"], 1)
            dve.wait_ge(k.sem["bias_step"], s.at("bias_step", key))

        dve.wait_ge(k.dma["bias_in"], self.done)
        step(dve.tensor_copy(k.bpos[:], k.bposi[:]), 0)
        step(dve.tensor_copy(k.brow[:], k.browi[:]), 1)
        step(dve.tensor_scalar(k.brow[:], k.brow[:], k.starts, None, ALU.subtract), 2)
        step(dve.tensor_tensor(k.btab[:, 0, :], k.btab[:, 0, :], k.btab[:, 1, :], ALU.subtract), 3)
        step(dve.memset(k.bdiag[:], 0.0), 4)
        for q in range(4):
            ins = dve.tensor_copy(k.bdiag[32 * q:32 * q + 32, HEADS * q:HEADS * (q + 1)],
                                  k.btab[32 * q:32 * q + 32, 0, :])
            if q in (2, 3):
                step(ins, 3 + q)
        if self.lam:
            for n in range(2):
                step(dve.tensor_tensor_reduce(k.lamv[:, 2 * n, :], k.lamv[:, 2 * n, :], k.lamv[:, 2 * n + 1, :], 1.0,
                                              0.0, ALU.mult, ALU.add, k.lams[:, n:n + 1]), 7 + n)
            dve.wait_ge(k.sem["bias_step"], s.at("bias_step", 9))
            step(dve.scalar_tensor_tensor(k.neg_lam[:], k.lams[:, 3:4], -LAM_INIT, k.lams[:, 2:3], ALU.add,
                                          ALU.subtract), 10)
        for e, b in zip(self.e, self.blocks):
            width = P * (b + 1)
            with dve.Fori(0, 4) as i:
                for n in range(8):
                    dve.wait_ge(k.sem["bias_mm"], e.at("bias_mm", n // 4, i, back=1))
                    group = i * 8 + (32 * b + n)
                    dve.tensor_scalar(k.bsel[:, n % 4, 0:width], k.bpos[:, 0:width], k.brow[:, bass.ds(group, 1)],
                                      None, ALU.is_le).then_inc(k.sem["bias_sel"], 1)


class Rope(Stage):

    def plan(self):
        self.done = self.k.moved("bias_in")
        self.e = self.k.events(1, rope_step=range(18))

    def inputs(self, act):
        k = self.k
        act.dma_start(k.sq[0][:].bitcast(I32), k.dram["pos"].to_broadcast([P, T])).then_inc(k.dma["bias_in"], 16)

    def vector(self, dve):
        k = self.k
        count = [0]

        def step(ins):
            ins.then_inc(k.sem["rope_step"], 1)
            dve.wait_ge(k.sem["rope_step"], self.e.at("rope_step", count[0]))
            count[0] += 1

        turn = 2 * math.pi
        part1 = 6.28125
        part2 = float(np.float32(round((turn - part1) * 2 ** 21) / 2 ** 21))
        part3 = float(np.float32(turn - part1 - part2))
        whole = 1.5 * 2 ** 23
        angle, turns = k.tmp[0][:], k.tmp[1][:]
        dve.wait_ge(k.dma["bias_in"], self.done)
        step(dve.tensor_copy(k.tmp[2][:], k.sq[0][:].bitcast(I32)))
        step(dve.tensor_scalar(angle, k.tmp[2][:], k.inv_freq, None, ALU.mult))
        for dst, shift in ((k.sin[:], 0.0), (k.cos[:], 0.25)):
            step(dve.tensor_scalar(turns, angle, 1.0 / turn, shift, ALU.mult, ALU.add))
            step(dve.tensor_scalar(turns, turns, whole, None, ALU.add))
            step(dve.tensor_scalar(turns, turns, -whole, None, ALU.add))
            step(dve.scalar_tensor_tensor(dst, turns, -part1, angle, ALU.mult, ALU.add))
            step(dve.scalar_tensor_tensor(dst, turns, -part2, dst, ALU.mult, ALU.add))
            step(dve.scalar_tensor_tensor(dst, turns, -part3, dst, ALU.mult, ALU.add))
            if shift:
                step(dve.tensor_scalar(dst, dst, shift * turn, None, ALU.add))
            step(dve.tensor_scalar(dst, dst, 3.1415925, -3.1415925, ALU.min, ALU.max))
        assert count[0] == 17

    def scalar(self, act):
        k = self.k
        act.wait_ge(k.sem["rope_step"], self.e.at("rope_step", 16))
        act.activation(k.sin[:], k.sin[:], ACT.Sin)
        act.activation(k.cos[:], k.cos[:], ACT.Sin).then_inc(k.sem["rope_step"], 1)


class Latent(Stage):

    def __init__(self, k, weights, n, gain, hi, lo, keys, after):
        self.weights, self.n, self.gain, self.hi, self.lo, self.keys = k.dram[weights], n, gain, hi, lo, keys
        super().__init__(k, after)

    def plan(self):
        n = self.n
        self.rs = self.k.lat[:, 3, :] if self.keys else self.k.rs[:]
        self.w = self.k.slots([SLOT] * n + ([4 * P] * 2 if self.keys else []), 1)
        sums = range(2 if self.keys else 1)
        self.e = self.k.events(1, norm_sq=range(n + (1 if self.keys else 0)), norm_sum=sums, norm_log=sums,
                               norm_rstd=sums, scaled=range(n), x_hi=range(n), x_lo=range(n),
                               **(dict(norm_out=range(4), rope_rot=[0]) if self.keys else {}))

    def sync(self, sp):
        for pos in range(self.n):
            self.k.load(sp, self.w, 0, pos, self.weights[pos])
        if self.keys:
            for q in range(2):
                self.k.load(sp, self.w, 0, self.n + q, self.weights[self.n, :, 4 * P * q:4 * P * (q + 1)])

    def tensor(self, pe):
        k, e, n = self.k, self.e, self.n
        for pos in range(n):
            k.panel(pe, self.w, 0, pos, k.ps[:, pos, :], k.xh, k.xl, ready=self.x_ready if pos == 0 else None)
        if self.keys:
            for q in range(2):
                k.panel(pe, self.w, 0, n + q, k.ps[:, n, :], k.xh, k.xl, k0=4 * q, nk=4, first=q == 0, last=q == 1)
        for m in range(n):
            pe.wait_ge(k.sem["norm_sq"], e.at("norm_sq", m))
            mm = pe.matmul(k.ps[:, 7, :], k.ones, k.tmp[m][:], start=m == 0, stop=m == n - 1)
        mm.then_inc(k.sem["norm_sum"], 1)
        if self.keys:
            pe.wait_ge(k.sem["norm_sq"], e.at("norm_sq", n))
            pe.matmul(k.ps[:, 6, :], k.half_ones, k.tmp[n][:], start=True, stop=True).then_inc(k.sem["norm_sum"], 1)
            pe.wait_ge(k.sem["norm_out"], e.at("norm_out", 0))
            pe.matmul(k.ps[:, 5, :], k.rot, k.kpe[:], start=True, stop=True).then_inc(k.sem["rope_rot"], 1)

    def scalar(self, act):
        k, e, n = self.k, self.e, self.n
        act.preload_act_table_set("natural_log_exp_and_others")
        for pos in range(n + (1 if self.keys else 0)):
            act.wait_ge(k.sem["slot_used"], self.w.used(0, pos + (1 if pos == n else 0)))
            act.activation(k.tmp[pos][:], k.ps[:, pos, :], ACT.Square).then_inc(k.sem["norm_sq"], 1)
        for m, (bank, width, dst) in enumerate(((7, n * P, self.rs), (6, 64, k.acc[:]))[0:2 if self.keys else 1]):
            act.wait_ge(k.sem["norm_sum"], e.at("norm_sum", m))
            act.activation(k.sq[m][:], k.ps[:, bank, :], ACT.Ln, bias=k.eps, scale=1.0 / width
                           ).then_inc(k.sem["norm_log"], 1)
            act.wait_ge(k.sem["norm_log"], e.at("norm_log", m))
            act.activation(dst, k.sq[m][:], ACT.Exp, scale=-0.5).then_inc(k.sem["norm_rstd"], 1)
        for m in range(n):
            act.wait_ge(k.sem["scaled"], e.at("scaled", m))
            act.activation(self.hi[:, m, :], k.lat[:, m, :], ACT.Copy).then_inc(k.sem["x_hi"], 1)

    def vector(self, dve):
        k, e, n = self.k, self.e, self.n
        for pos in range(len(self.w.sizes)):
            k.round_hi(dve, self.w, 0, pos + 2)
        dve.wait_ge(k.sem["norm_rstd"], e.at("norm_rstd", 0))
        for m in range(n):
            dve.scalar_tensor_tensor(k.lat[:, m, :], k.ps[:, m, :], k.vecs[:, self.gain + m:self.gain + m + 1],
                                     self.rs, ALU.mult, ALU.mult).then_inc(k.sem["scaled"], 1)
        if self.keys:
            g = k.V["k_pe_norm"]
            dve.wait_ge(k.sem["norm_rstd"], e.at("norm_rstd", 1))
            dve.scalar_tensor_tensor(k.kpe[:], k.ps[:, n, :], k.vecs[:, g:g + 1], k.acc[:], ALU.mult, ALU.mult
                                     ).then_inc(k.sem["norm_out"], 1)
            dve.wait_ge(k.sem["rope_rot"], e.at("rope_rot"))
            dve.tensor_tensor(k.tmp[0][:], k.ps[:, 5, :], k.sin[:], ALU.mult).then_inc(k.sem["norm_out"], 1)
            dve.tensor_tensor(k.kpe[:], k.kpe[:], k.cos[:], ALU.mult).then_inc(k.sem["norm_out"], 1)
            dve.wait_ge(k.sem["norm_out"], e.at("norm_out", 2))
            dve.tensor_tensor(k.kpe[:], k.kpe[:], k.tmp[0][:], ALU.add).then_inc(k.sem["norm_out"], 1)

    def gpsimd(self, pool):
        k, e = self.k, self.e
        for pos in range(len(self.w.sizes)):
            k.take_lo(pool, self.w, 0, pos + 2)
        for m in range(self.n):
            pool.wait_ge(k.sem["x_hi"], e.at("x_hi", m))
            pool.tensor_tensor(self.lo[:, m, :], k.lat[:, m, :], self.hi[:, m, :].bitcast(F32), ALU.subtract
                               ).then_inc(k.sem["x_lo"], 1)


class DiffHeads(Stage):
    ROUNDS = HEADS // 2
    Q_BANK, K_BANK, V_BANK = (0, 3), (1, 4), (2, 5)

    def plan(self):
        self.weights = self.k.dram["diff"]
        self.w = self.k.slots([SLOT] * 6, self.ROUNDS)
        u, m, two = range(8), range(16), range(2)
        self.e = self.k.events(self.ROUNDS, norm_sq=range(6), norm_sum=range(6), norm_log=range(6),
                               norm_rstd=range(6), norm_out=range(6), hg_v=two, hg_turn=two, hg_turn_out=two,
                               logits=m, row_min=m, probs_raw=m, row_recip=u, scaled=u, probs=u, probs_t=u,
                               probs_t_out=u, pv=two, y_hi=two, y_lo=two)
        self.tile_base = [self.k.moved(f"tile_in{j}", 4 * self.ROUNDS) - 64 * self.ROUNDS for j in range(2)]

    def a_made(self, t):
        return self.of_tile("y_lo", t, 2)

    def bank_read(self, j):
        return self.last("row_min", 15)

    def sync(self, sp):
        k, e = self.k, self.e
        with sp.Fori(0, self.ROUNDS) as i:
            for pos in range(6):
                k.load(sp, self.w, i, pos, self.weights[6 * i + pos])

    def tensor(self, pe):
        k, e = self.k, self.e

        def norm_sum(n):
            pe.wait_ge(k.sem["norm_sq"], e.at("norm_sq", n, i))
            pe.wait_ge(k.sem["norm_log"], e.at("norm_log", n, i, back=1))
            pe.matmul(k.ps[:, 7, :], k.half_ones if n < 4 else k.ones, k.sq[n % 2][:], start=True, stop=True
                      ).then_inc(k.sem["norm_sum"], 1)

        def turn_values(j):
            pe.wait_ge(k.sem["hg_v"], e.at("hg_v", j, i))
            if j == 0:
                pe.wait_ge(k.sem["norm_out"], e.before("norm_out", 5, i))
            else:
                pe.wait_ge(k.sem["hg_turn_out"], e.at("hg_turn_out", 0, i))
            for b in range(NB):
                mm = pe.transpose(k.ps[:, 6, b * P:(b + 1) * P], k.dvt[:, b * P:(b + 1) * P], k.ident)
            mm.then_inc(k.sem["hg_turn"], 1)

        def transposes(n):
            j, b = n // 4, n % 4
            pe.wait_ge(k.sem["probs"], e.at("probs", n, i))
            pe.wait_ge(k.sem["probs_t_out"], e.at("probs_t_out", n, i, back=2))
            for s in range(b + 1):
                mm = pe.transpose(k.ps[:, 4 + n % 2, s * P:(s + 1) * P], k.dw[:, n % 2, s * P:(s + 1) * P], k.ident)
            mm.then_inc(k.sem["probs_t"], 1)
            if b == 3:
                pe.wait_ge(k.sem["probs_t_out"], e.at("probs_t_out", n, i))
                if j == 0:
                    pe.wait_ge(k.sem["hg_turn_out"], e.at("hg_turn_out", 1, i))
                else:
                    pe.wait_ge(k.sem["norm_out"], e.at("norm_out", 4, i))
                for s in range(NB):
                    mm = pe.matmul(k.ps[:, 6, s * P:T], k.dvr[:, j, s, :], k.dpt[:, j, s, s * P:T],
                                   start=s == 0, stop=s == NB - 1)
                mm.then_inc(k.sem["pv"], 1)

        with pe.Fori(0, self.ROUNDS) as i:
            pe.wait_ge(k.sem["row_min"], e.before("row_min", 15, i))
            pe.wait_ge(k.sem["probs_t_out"], e.before("probs_t_out", 7, i))
            for pos in range(6):
                k.panel(pe, self.w, i, pos, k.ps[:, pos, :], k.xh, k.xl, ready=self.x_ready if pos == 0 else None)
                {1: norm_sum, 2: norm_sum, 4: norm_sum, 5: norm_sum}.get(pos, lambda n: None)(
                    {1: 0, 2: 1, 4: 2, 5: 3}.get(pos))
                if pos == 3:
                    turn_values(0)
            turn_values(1)
            for n in range(8 + 2):
                if n < 8:
                    j, b = n // 4, n % 4
                    if n == 0:
                        pe.wait_ge(k.sem["norm_out"], e.at("norm_out", 3, i))
                        pe.wait_ge(k.sem["hg_v"], e.at("hg_v", 1, i))
                    for c in range(2):
                        m = 2 * n + c
                        if n >= 2:
                            pe.wait_ge(k.sem["row_min"], e.at("row_min", m - 4, i))
                        bank = k.ps[:, 2 * (n % 2) + c, :]
                        pe.matmul(bank[:, 0:P * (b + 1)], k.dq[64 * c:64 * c + 64, j, b * P:(b + 1) * P],
                                  k.dk[64 * c:64 * c + 64, j, 0:P * (b + 1)], start=True, stop=False)
                        pe.matmul(bank[:, P * b:P * (b + 1)], k.ident_b, k.causal_b, start=False, stop=True
                                  ).then_inc(k.sem["logits"], 1)
                if n >= 2:
                    transposes(n - 2)
                if n == 7:
                    norm_sum(4)
            norm_sum(5)

    def scalar(self, act):
        k, e = self.k, self.e
        act.preload_act_table_set("natural_log_exp_and_others")

        def square(n, bank):
            act.wait_ge(k.sem["norm_sum"], e.at("norm_sum", n, i, back=2))
            act.activation(k.sq[n % 2][:], k.ps[:, bank, :], ACT.Square).then_inc(k.sem["norm_sq"], 1)

        def rstd(n):
            act.wait_ge(k.sem["norm_sum"], e.at("norm_sum", n, i))
            act.wait_ge(k.sem["norm_rstd"], e.at("norm_rstd", n, i, back=1))
            act.wait_ge(k.sem["norm_out"], e.at("norm_out", n, i, back=2))
            act.activation(k.acc[:], k.ps[:, 7, :], ACT.Ln, bias=k.eps, scale=1.0 / (64 if n < 4 else P)
                           ).then_inc(k.sem["norm_log"], 1)
            act.wait_ge(k.sem["norm_log"], e.at("norm_log", n, i))
            extra = dict(bias=k.log_keep) if n >= 4 else dict(bias=k.log_att_scale) if n % 2 == 0 else {}
            act.activation(k.tmp[n % 2][:], k.acc[:], ACT.Exp, scale=-0.5, **extra).then_inc(k.sem["norm_rstd"], 1)

        def values(j):
            act.wait_ge(k.sem["slot_used"], self.w.used(i, 3 * j + 2))
            act.wait_ge(k.sem["hg_turn"], e.at("hg_turn", j, i, back=1))
            act.activation(k.dvt[:], k.ps[:, self.V_BANK[j], :], ACT.Copy).then_inc(k.sem["hg_v"], 1)

        def value_rows(j):
            act.wait_ge(k.sem["hg_turn"], e.at("hg_turn", j, i))
            act.activation(k.dvr[:, j].rearrange("p b v -> p (b v)"), k.ps[:, 6, :], ACT.Copy
                           ).then_inc(k.sem["hg_turn_out"], 1)

        def turned_out(n):
            j, b = n // 4, n % 4
            act.wait_ge(k.sem["probs_t"], e.at("probs_t", n, i))
            act.activation(k.dpt[:, j, 0:b + 1, b * P:(b + 1) * P],
                           k.ps[:, 4 + n % 2, 0:P * (b + 1)].rearrange("p (s q) -> p s q", q=P), ACT.Copy
                           ).then_inc(k.sem["probs_t_out"], 1)

        def output_hi(j):
            act.wait_ge(k.sem["norm_out"], e.at("norm_out", 4 + j, i))
            act.activation(k.oh[:, 2 * i + j, :], k.tmp[2 + j][:], ACT.Copy).then_inc(k.sem["y_hi"], 1)

        bias = k.dram["bias"].rearrange("(b q h) s -> h b q s", h=HEADS, q=P)
        with act.Fori(0, self.ROUNDS) as i:
            for j in range(2):
                act.wait_ge(k.sem["row_min"], e.before("row_min", 8 * j + 7, i))
                for b in range(NB):
                    act.dma_start(k.dbias[:, j, TRI[b]:TRI[b + 1]], bias[2 * i + j, b, :, 0:P * (b + 1)]
                                  ).then_inc(k.dma[f"tile_in{j}"], 16)
            act.wait_ge(k.sem["pv"], e.before("pv", 1, i))
            for j in range(2):
                for g in range(2):
                    act.wait_ge(k.sem["slot_used"], self.w.used(i, 3 * j + g))
                    square(2 * j + g, 3 * j + g)
                rstd(2 * j)
                values(j)
                rstd(2 * j + 1)
                value_rows(j)
            for n in range(8 + 2):
                if n < 8:
                    b = n % 4
                    for c in range(2):
                        m = 2 * n + c
                        tile = k.de[:, 2 * (n % 2) + c, 0:P * (b + 1)]
                        act.wait_ge(k.sem["row_min"], e.at("row_min", m, i))
                        act.activation(tile, tile, ACT.Exp, bias=k.small[:, m:m + 1], scale=-1.0,
                                       accum_out=k.small[:, 16 + m:17 + m]).then_inc(k.sem["probs_raw"], 1)
                if n >= 2:
                    turned_out(n - 2)
                if n in (6, 9):
                    j = 0 if n == 6 else 1
                    act.wait_ge(k.sem["pv"], e.at("pv", j, i))
                    square(4 + j, 6)
                if n == 8:
                    rstd(4)
                    output_hi(0)
            rstd(5)
            output_hi(1)

    def vector(self, dve):
        k, e, V = self.k, self.e, self.k.V

        def norm_out(n):
            dve.wait_ge(k.sem["norm_rstd"], e.at("norm_rstd", n, i))
            if n < 4:
                dst, gain, bank = (k.dq, k.dk)[n % 2][:, n // 2, :], (V["a_q_norm"], V["a_k_norm"])[n % 2], \
                    3 * (n // 2) + n % 2
            else:
                dst, gain, bank = k.tmp[n - 2][:], V["a_sub_norm"], 6
                dve.wait_ge(k.sem["y_lo"], e.before("y_lo", n - 4, i))
            dve.scalar_tensor_tensor(dst, k.ps[:, bank, :], k.vecs[:, gain:gain + 1], k.tmp[n % 2][:],
                                     ALU.mult, ALU.mult).then_inc(k.sem["norm_out"], 1)

        def combine(n):
            b = n % 4
            width = P * (b + 1)
            two = k.small[:, 16 + 2 * n:18 + 2 * n]
            dve.wait_ge(k.sem["probs_raw"], e.at("probs_raw", 2 * n + 1, i))
            dve.reciprocal(k.small[:, 32 + 2 * n:34 + 2 * n], two).then_inc(k.sem["row_recip"], 1)
            dve.wait_ge(k.sem["row_recip"], e.at("row_recip", n, i))
            dve.wait_ge(k.sem["probs_t"], e.at("probs_t", n, i, back=2))
            w = k.dw[:, n % 2, 0:width]
            dve.tensor_scalar(w, k.de[:, 2 * (n % 2) + 1, 0:width], k.small[:, 33 + 2 * n:34 + 2 * n], k.neg_lam[:],
                              ALU.mult, ALU.mult).then_inc(k.sem["scaled"], 1)
            dve.wait_ge(k.sem["scaled"], e.at("scaled", n, i))
            dve.scalar_tensor_tensor(w, k.de[:, 2 * (n % 2), 0:width], k.small[:, 32 + 2 * n:33 + 2 * n], w,
                                     ALU.mult, ALU.add).then_inc(k.sem["probs"], 1)

        with dve.Fori(0, self.ROUNDS) as i:
            for j in range(2):
                for pos in range(3 * j, 3 * j + 3):
                    k.round_hi(dve, self.w, i, pos + 2)
                if j == 1:
                    norm_out(0)
                    norm_out(1)
            norm_out(2)
            norm_out(3)
            for n in range(8 + 1):
                if n < 8:
                    j, b = n // 4, n % 4
                    if b == 0:
                        dve.wait_ge(k.dma[f"tile_in{j}"], i * 64 + (self.tile_base[j] + 64))
                    for c in range(2):
                        m = 2 * n + c
                        dve.wait_ge(k.sem["logits"], e.at("logits", m, i))
                        dve.wait_ge(k.sem["probs"], e.at("probs", n, i, back=2))
                        k.carry(dve)
                        dve.tensor_tensor_reduce(k.de[:, 2 * (n % 2) + c, 0:P * (b + 1)],
                                                 k.ps[:, 2 * (n % 2) + c, 0:P * (b + 1)],
                                                 k.dbias[:, j, TRI[b]:TRI[b + 1]], -1.0, 3e38, ALU.add, ALU.min,
                                                 k.small[:, m:m + 1]).then_inc(k.sem["row_min"], 1)
                if n >= 1:
                    combine(n - 1)
            norm_out(4)
            norm_out(5)

    def gpsimd(self, pool):
        k, e = self.k, self.e
        with pool.Fori(0, self.ROUNDS) as i:
            for pos in range(6):
                k.take_lo(pool, self.w, i, pos + 2)
            for j in range(2):
                pool.wait_ge(k.sem["y_hi"], e.at("y_hi", j, i))
                pool.tensor_tensor(k.ol[:, 2 * i + j, :], k.tmp[2 + j][:], k.oh[:, 2 * i + j, :].bitcast(F32),
                                   ALU.subtract).then_inc(k.sem["y_lo"], 1)


class MlaHeads(Stage):
    ROUNDS = 4

    def __init__(self, k, half, after=None):
        self.weights, self.weights_pe, self.half = k.dram["mla"], k.dram["mla_pe"], half
        super().__init__(k, after)

    def plan(self):
        self.w = self.k.slots([SLOT, SLOT, 2 * P, 2 * P], self.ROUNDS)
        u, two, five = range(8), range(2), range(5)
        self.e = self.k.events(self.ROUNDS, product=range(6), norm_sq=five, norm_sum=five, norm_log=five,
                               norm_rstd=five, norm_out=range(8), rope_rot=[0], hg_v=two, hg_turn=two,
                               hg_turn_out=two, logits=u, row_min=u, probs_raw=u, row_recip=u, probs=u, probs_t=u,
                               probs_t_out=u, pv=two, y_hi=two, y_lo=two)

    def a_made(self, t):
        return self.of_tile("y_lo", t, 2)

    def bank_read(self, j):
        return self.last("probs_t_out", 7)

    def sync(self, sp):
        with sp.Fori(0, self.ROUNDS) as i:
            for j in range(2):
                self.k.load(sp, self.w, i, j, self.weights[2 * i + (8 * self.half + j)])
            for q in range(2):
                self.k.load(sp, self.w, i, 2 + q, self.weights_pe[i + 4 * self.half, :, 2 * P * q:2 * P * (q + 1)])

    def tensor(self, pe):
        k, e = self.k, self.e

        def norm_sum(n):
            pe.wait_ge(k.sem["norm_sq"], e.at("norm_sq", n, i))
            pe.wait_ge(k.sem["norm_log"], e.at("norm_log", n, i, back=1))
            pe.matmul(k.ps[:, 7, :], k.half_ones if n == 4 else k.ones, k.tmp[n % 2][:], start=True, stop=True
                      ).then_inc(k.sem["norm_sum"], 1)

        def turn_values(j):
            pe.wait_ge(k.sem["hg_v"], e.at("hg_v", j, i))
            pe.wait_ge(k.sem["norm_log"], e.at("norm_log", 4, i))
            if j:
                pe.wait_ge(k.sem["hg_turn_out"], e.at("hg_turn_out", 0, i))
            for b in range(NB):
                mm = pe.transpose(k.ps[:, 7, b * P:(b + 1) * P], k.mvt[:, b * P:(b + 1) * P], k.ident)
            mm.then_inc(k.sem["hg_turn"], 1)

        def transposes(n):
            j, b = n // 4, n % 4
            pe.wait_ge(k.sem["probs"], e.at("probs", n, i))
            pe.wait_ge(k.sem["probs_t_out"], e.at("probs_t_out", n, i, back=2))
            for s in range(b + 1):
                mm = pe.transpose(k.ps[:, 3 + n % 2, s * P:(s + 1) * P], k.me[:, n % 3, s * P:(s + 1) * P], k.ident)
            mm.then_inc(k.sem["probs_t"], 1)
            if b == 3:
                pe.wait_ge(k.sem["probs_t_out"], e.at("probs_t_out", n, i))
                for s in range(NB):
                    mm = pe.matmul(k.ps[:, 5 + j, s * P:T], k.mvr[:, j, s, :], k.mpt[:, j, s, s * P:T],
                                   start=s == 0, stop=s == NB - 1)
                mm.then_inc(k.sem["pv"], 1)

        with pe.Fori(0, self.ROUNDS) as i:
            if self.after is not None:
                pe.wait_ge(*self.after.last("added", 3))
            pe.wait_ge(k.sem["y_lo"], e.before("y_lo", 1, i))
            pe.wait_ge(k.sem["probs_t_out"], e.before("probs_t_out", 7, i))
            pe.wait_ge(k.sem["hg_turn_out"], e.before("hg_turn_out", 1, i))
            for j in range(2):
                for g, (x, nk, col) in enumerate((((k.cqh, k.cql), 4, 0), ((k.ckh, k.ckl), 2, 4 * P),
                                                  ((k.ckh, k.ckl), 2, 6 * P))):
                    k.panel(pe, self.w, i, j, k.ps[:, 3 * j + g, :], *x, nk=nk, col=col, done=False
                            ).then_inc(k.sem["product"], 1)
                pe.wait_ge(k.sem["product"], e.at("product", 3 * j + 2, i))
                pe.sem_inc(k.sem["slot_used"], 1)
            for q in range(2):
                k.panel(pe, self.w, i, 2 + q, k.ps[:, 6, :], k.cqh, k.cql, k0=2 * q, nk=2, first=q == 0, last=q == 1)
            for n in range(5):
                norm_sum(n)
            turn_values(0)
            turn_values(1)
            pe.wait_ge(k.sem["norm_out"], e.at("norm_out", 4, i))
            pe.matmul(k.ps[:, 6, :], k.rot, k.qpe[:], start=True, stop=True).then_inc(k.sem["rope_rot"], 1)
            for n in range(8 + 2):
                if n < 8:
                    j, b = n // 4, n % 4
                    if n == 0:
                        pe.wait_ge(k.sem["norm_out"], e.at("norm_out", 7, i))
                        pe.wait_ge(k.sem["hg_v"], e.at("hg_v", 1, i))
                    if n >= 3:
                        pe.wait_ge(k.sem["probs_raw"], e.at("probs_raw", n - 3, i))
                    bank = k.ps[:, n % 3, :]
                    pe.matmul(bank[:, 0:P * (b + 1)], k.mq[:, j, b * P:(b + 1) * P], k.mk[:, j, 0:P * (b + 1)],
                              start=True, stop=False)
                    pe.matmul(bank[:, 0:P * (b + 1)], k.qpe[64 * j:64 * j + 64, b * P:(b + 1) * P],
                              k.kpe[64 * j:64 * j + 64, 0:P * (b + 1)], start=False, stop=False)
                    pe.matmul(bank[:, P * b:P * (b + 1)], k.ident_b, k.causal_b, start=False, stop=True
                              ).then_inc(k.sem["logits"], 1)
                if n >= 2:
                    transposes(n - 2)

    def scalar(self, act):
        k, e = self.k, self.e
        act.preload_act_table_set("natural_log_exp_and_others")
        norms = ((0, P), (1, P), (3, P), (4, P), (6, 64))

        def square(n):
            act.wait_ge(k.sem["norm_sum"], e.at("norm_sum", n, i, back=2))
            act.activation(k.tmp[n % 2][:], k.ps[:, norms[n][0], :], ACT.Square).then_inc(k.sem["norm_sq"], 1)

        def rstd(n):
            act.wait_ge(k.sem["norm_sum"], e.at("norm_sum", n, i))
            act.wait_ge(k.sem["norm_rstd"], e.at("norm_rstd", n, i, back=1))
            act.wait_ge(k.sem["norm_out"], e.at("norm_out", n, i, back=2) if n >= 2 else e.before("norm_out", 7, i))
            act.activation(k.acc[:], k.ps[:, 7, :], ACT.Ln, bias=k.eps, scale=1.0 / norms[n][1]
                           ).then_inc(k.sem["norm_log"], 1)
            act.wait_ge(k.sem["norm_log"], e.at("norm_log", n, i))
            extra = dict(bias=k.log_scale) if n in (0, 2, 4) else {}
            act.activation(k.tmp[2 + n % 2][:], k.acc[:], ACT.Exp, scale=-0.5, **extra
                           ).then_inc(k.sem["norm_rstd"], 1)

        def values(j):
            act.wait_ge(k.sem["product"], e.at("product", 3 * j + 2, i))
            act.wait_ge(k.sem["hg_turn"], e.at("hg_turn", j, i, back=1))
            act.activation(k.mvt[:], k.ps[:, 3 * j + 2, :], ACT.Copy).then_inc(k.sem["hg_v"], 1)

        def value_rows(j):
            act.wait_ge(k.sem["hg_turn"], e.at("hg_turn", j, i))
            act.activation(k.mvr[:, j].rearrange("p b v -> p (b v)"), k.ps[:, 7, :], ACT.Copy
                           ).then_inc(k.sem["hg_turn_out"], 1)

        def turned_out(n):
            j, b = n // 4, n % 4
            act.wait_ge(k.sem["probs_t"], e.at("probs_t", n, i))
            act.activation(k.mpt[:, j, 0:b + 1, b * P:(b + 1) * P],
                           k.ps[:, 3 + n % 2, 0:P * (b + 1)].rearrange("p (s q) -> p s q", q=P), ACT.Copy
                           ).then_inc(k.sem["probs_t_out"], 1)

        def output_hi(j):
            act.wait_ge(k.sem["pv"], e.at("pv", j, i))
            act.activation(k.xh[:, 2 * i + j, :], k.ps[:, 5 + j, :], ACT.Copy).then_inc(k.sem["y_hi"], 1)

        with act.Fori(0, self.ROUNDS) as i:
            act.wait_ge(k.sem["pv"], e.before("pv", 1, i))
            for n in range(2):
                act.wait_ge(k.sem["product"], e.at("product", n, i))
                square(n)
            values(0)
            for n in range(2, 4):
                act.wait_ge(k.sem["product"], e.at("product", n + 1, i))
                rstd(n - 2)
                square(n)
            act.wait_ge(k.sem["slot_used"], self.w.used(i, 3))
            rstd(2)
            square(4)
            rstd(3)
            rstd(4)
            value_rows(0)
            values(1)
            value_rows(1)
            for n in range(8 + 2):
                if n < 8:
                    b = n % 4
                    act.wait_ge(k.sem["row_min"], e.at("row_min", n, i))
                    act.wait_ge(k.sem["probs_t"], e.at("probs_t", n, i, back=3))
                    act.activation(k.me[:, n % 3, 0:P * (b + 1)], k.ps[:, n % 3, 0:P * (b + 1)], ACT.Exp,
                                   bias=k.small[:, n:n + 1], accum_out=k.small[:, 16 + n:17 + n]
                                   ).then_inc(k.sem["probs_raw"], 1)
                if n >= 2:
                    turned_out(n - 2)
                if n == 6:
                    output_hi(0)
            output_hi(1)

    def vector(self, dve):
        k, e, V = self.k, self.e, self.k.V
        qg, kg, pg = V["b_q_nope_norm"], V["k_nope_norm"], V["b_q_pe_norm"]
        outs = ((k.mq[:, 0, :], qg, 0), (k.mk[:, 0, :], kg, 1), (k.mq[:, 1, :], qg, 3), (k.mk[:, 1, :], kg, 4),
                (k.qpe[:], pg, 6))

        def norm_out(n):
            dst, gain, bank = outs[n]
            dve.wait_ge(k.sem["norm_rstd"], e.at("norm_rstd", n, i))
            dve.scalar_tensor_tensor(dst, k.ps[:, bank, :], k.vecs[:, gain:gain + 1], k.tmp[2 + n % 2][:],
                                     ALU.mult, ALU.mult).then_inc(k.sem["norm_out"], 1)

        def normalize(n):
            b = n % 4
            dve.wait_ge(k.sem["probs_raw"], e.at("probs_raw", n, i))
            dve.reciprocal(k.small[:, 32 + n:33 + n], k.small[:, 16 + n:17 + n]).then_inc(k.sem["row_recip"], 1)
            dve.wait_ge(k.sem["row_recip"], e.at("row_recip", n, i))
            tile = k.me[:, n % 3, 0:P * (b + 1)]
            dve.tensor_scalar(tile, tile, k.small[:, 32 + n:33 + n], None, ALU.mult).then_inc(k.sem["probs"], 1)

        def low(j):
            dve.wait_ge(k.sem["y_hi"], e.at("y_hi", j, i))
            dve.tensor_tensor(k.xl[:, 2 * i + j, :], k.ps[:, 5 + j, :], k.xh[:, 2 * i + j, :].bitcast(F32),
                              ALU.subtract).then_inc(k.sem["y_lo"], 1)

        with dve.Fori(0, self.ROUNDS) as i:
            for pos in range(4):
                k.round_hi(dve, self.w, i, pos + 2)
            for n in range(5):
                norm_out(n)
            dve.wait_ge(k.sem["rope_rot"], e.at("rope_rot", 0, i))
            dve.tensor_tensor(k.rs[:], k.ps[:, 6, :], k.sin[:], ALU.mult).then_inc(k.sem["norm_out"], 1)
            dve.tensor_tensor(k.qpe[:], k.qpe[:], k.cos[:], ALU.mult).then_inc(k.sem["norm_out"], 1)
            dve.wait_ge(k.sem["norm_out"], e.at("norm_out", 6, i))
            dve.tensor_tensor(k.qpe[:], k.qpe[:], k.rs[:], ALU.add).then_inc(k.sem["norm_out"], 1)
            for n in range(8 + 1):
                if n < 8:
                    b = n % 4
                    dve.wait_ge(k.sem["logits"], e.at("logits", n, i))
                    dve.tensor_reduce(k.small[:, n:n + 1], k.ps[:, n % 3, 0:P * (b + 1)], AX.X, ALU.max, negate=True
                                      ).then_inc(k.sem["row_min"], 1)
                if n >= 1:
                    normalize(n - 1)
                if n == 7:
                    low(0)
            low(1)

    def gpsimd(self, pool):
        with pool.Fori(0, self.ROUNDS) as i:
            for pos in range(4):
                self.k.take_lo(pool, self.w, i, pos + 2)


class StoreResult(Stage):
    def sync(self, sp):
        k = self.k
        k.meet(sp, self.number)
        sp.dma_start(k.dram["out"], k.h[:].rearrange("p a t -> p (a t)")).then_inc(k.dma["stored"], 16)


def build_stages(k, V):
    s = [Setup(k)]

    def add(stage):
        s.append(stage)
        return stage

    def swiglu(n, h=None):
        norm = add(PreNorm(k, V[n + "_pre_g"], after=h))
        up = add(SwigluUp(k, n + "_up", norm))
        down = add(OutProj(k, n + "_down", k.ah, k.al, KF, k.y_over_x, after=up))
        return add(Residual(k, k.y_over_x, V[n + "_post_g"], True, down))

    def conv_ffn(n, h):
        norm = add(PreNorm(k, V[f"ffn_norm{n}"], "summed", h))
        up = add(ConvUp(k, f"conv{n}_up", V[f"conv{n}"], norm))
        return add(OutProj(k, f"conv{n}_down", k.ah, k.al, KF, after=up))

    def ple(n, norm, h):
        split = add(PleSplit(k, f"p{n}", h))
        normed = add(PreNorm(k, V[norm], "square" if n == 0 else "summed", split, h))
        proj = add(PleProj(k, f"ple{n}_proj", normed, split))
        gate = add(PleGate(k, f"ple{n}_gate", n == 0, n < 2, proj))
        return add(Residual(k, k.y_ple, V["ple_post_g"], False, gate)) if n == 0 else gate

    add(BiasTable(k, "table0", "iota", "strip", [NB - 1], NB - 1, False))
    add(BiasTable(k, "table1", "pos", "bias", range(NB), 0, True))
    h = swiglu("ffn1")
    norm = add(PreNorm(k, V["mix_pre_g"], after=h))
    add(MixProj(k, norm))
    add(IdxScore(k))
    add(TopK(k))
    add(DsaHeads(k))
    add(Hgrn(k))
    merge = add(Merge(k))
    out = add(OutProj(k, "w_out", k.mh, k.ml, KD, k.y_mix, after=merge))
    h = add(Residual(k, k.y_mix, V["mix_post_g"], False, out))
    h = ple(0, "ple_pre_g", swiglu("ffn2", h))
    heads = add(DiffHeads(k, add(PreNorm(k, V["attn_norm0"], after=h))))
    h = add(OutProj(k, "a_w_o", k.oh, k.ol, HEADS, after=heads))
    h = ple(1, "ple_norm0", conv_ffn(0, h))
    add(Rope(k))
    keys_norm = add(PreNorm(k, V["kv_norm"], "summed", None, h))
    keys = add(Latent(k, "w_dkv", 2, V["ckv_norm"], k.ckh, k.ckl, True, keys_norm))
    norm = add(PreNorm(k, V["attn_norm1"], "again", keys))
    add(Latent(k, "w_dq", 4, V["b_cq_norm"], k.cqh, k.cql, False, norm))
    first = add(MlaHeads(k, 0))
    out = add(OutProj(k, "b_w_o0", k.xh, k.xl, 8, summed=False, after=first))
    second = add(MlaHeads(k, 1, out))
    h = add(OutProj(k, "b_w_o1", k.xh, k.xl, 8, after=second))
    ple(2, "ple_norm1", conv_ffn(1, h))
    return s


def program(nc, dram, V):
    ctx = ExitStack()
    with ctx:
        k = Kernel(nc, ctx, dram, V)
        stages = build_stages(k, V)
        store = StoreResult(k)
        first = next(s for s in stages if s.w)
        tail = k.slots([SLOT] * 2, 1)
        credited = [n for n in SEMS if n in k.totals]
        block = ctx.enter_context(nc.Block())

        @block.sync
        def _(sp):
            for n in credited:
                sp.sem_inc(k.sem[n], CREDIT)
            for r in range(2):
                sp.sem_inc(k.dma[f"bias_stored{r}"], 16)
            sp.sem_inc(k.sem["slot_split"], RAW_SLOTS)
            sp.sem_inc(k.sem["slot_used"], SPLIT_SLOTS)
            for s in stages:
                s.sync(sp)
            for pos in range(2):
                k.load(sp, tail, 0, pos, dram["ffn1_up"][pos])
            store.sync(sp)
            sp.wait_ge(k.dma["stored"], k.moved("stored"))

        def split_ahead(piece, eng, s):
            if s is first:
                for pos in range(SPLIT_SLOTS):
                    piece(eng, s.w, 0, pos)

        def begin(eng, s):
            if s.after is None and s.number:
                k.barrier(eng)
                k.meet(eng, s.number)

        @block.tensor
        def _(pe):
            for s in stages:
                begin(pe, s)
                s.tensor(pe)
            k.barrier(pe)

        @block.scalar
        def _(act):
            for s in stages:
                begin(act, s)
                s.inputs(act)
                s.scalar(act)
            k.barrier(act)

        @block.vector
        def _(dve):
            for s in stages:
                begin(dve, s)
                split_ahead(k.round_hi, dve, s)
                s.vector(dve)
            k.barrier(dve)

        @block.gpsimd
        def _(pool):
            for s in stages:
                begin(pool, s)
                split_ahead(k.take_lo, pool, s)
                s.gpsimd(pool)
            k.barrier(pool)


def _tiles(w):
    K, M = w.shape[0] // P, w.shape[1] // P
    return np.ascontiguousarray(w.reshape(K, P, M, P).transpose(2, 1, 0, 3)).reshape(M, P, K * P)


def _cols(v):
    return np.ascontiguousarray(np.reshape(v, (-1, P)).T)


def _turned(x):
    n = x.shape[1] // P
    return np.ascontiguousarray(x.reshape(T, n, P).transpose(2, 1, 0)).reshape(P, n * T)


def _constants():
    half = 32
    c = np.zeros((P, 4 * P + 7), np.float32)
    c[:, 0:P] = 1.0
    c[0:64, P:P + 64] = 1.0
    c[64:, P + 64:2 * P] = 1.0
    c[:, 2 * P:3 * P] = np.eye(P)
    for m in range(P):
        if m % 64 < half:
            c[m + half, 3 * P + m] = -1.0
        else:
            c[m - half, 3 * P + m] = 1.0
    c[:, 4 * P] = EPS
    c[:, 4 * P + 1] = math.log(0.5)
    freq = np.exp(np.float32(-math.log(10000.0)) * np.arange(half, dtype=np.float32) * np.float32(2.0 / 64))
    c[:, 4 * P + 2] = np.tile(freq.astype(np.float32), 4)
    starts = np.array(bucket_starts(), np.float32)
    starts[0] = -1e9
    c[:, 4 * P + 3] = np.tile(starts, 4)
    c[:, 4 * P + 4] = math.log(1.0 - LAM_INIT)
    c[:, 4 * P + 5] = -0.5 * math.log(128 + 64)
    c[:, 4 * P + 6] = math.log(ATT_SCALE)
    return c


def kernel(**inputs):
    import ml_dtypes
    import concourse.bacc as bacc
    from concourse.bass_utils import run_bass_kernel_spmd

    a = {n: np.asarray(v) for n, v in inputs.items()}
    arrays = {"x": _turned(a["x"][0]), "consts": _constants()}
    m = np.zeros((P, 2 * P), ml_dtypes.bfloat16)
    m[:, 0:P] = np.eye(P)
    m[:, P:] = np.where(np.arange(P)[None, :] <= np.arange(P)[:, None], 0.0, NEG)
    arrays["maskc"] = m
    V, cols = {}, []

    def vec(name, v):
        V[name] = sum(c.shape[1] for c in cols)
        cols.append(_cols(v))

    for n in ("ffn1_pre_g", "ffn1_post_g", "mix_pre_g", "mix_post_g", "ffn2_pre_g", "ffn2_post_g",
              "ple_pre_g", "ple_post_g"):
        vec(n, a[n][0])
    for n in range(2):
        vec(f"ffn_norm{n}", a["ffn_norm_2"][n])
        vec(f"ple_norm{n}", a["ple_norm_2"][n])
        vec(f"attn_norm{n}", a["attn_norm_2"][n])
        taps = np.concatenate([a["ffn_conv_w_2"][n], a["ffn_conv_b_2"][n][None]]).reshape(4, 2, KF, P)
        vec(f"conv{n}", taps.transpose(2, 1, 0, 3))

    for n in ("ffn1", "ffn2"):
        arrays[n + "_up"] = np.stack([_tiles(a[n + "_w_gate"][0]), _tiles(a[n + "_w_up"][0])], 1
                                     ).reshape(2 * KF, P, D)
        arrays[n + "_down"] = _tiles(a[n + "_w_down"][0])
    for n in range(2):
        arrays[f"conv{n}_up"] = np.ascontiguousarray(
            _tiles(a["ffn_w_in_2"][n]).reshape(2, KF, P, D).transpose(1, 0, 2, 3)).reshape(2 * KF, P, D)
        arrays[f"conv{n}_down"] = _tiles(a["ffn_w_out_2"][n])
    ple = [(a["p"][0, 0], a["w_ple_proj"][0], a["w_ple_gate"][0])] + [
        (a["p_2"][n, 0], a["ple_w_proj_2"][n], a["ple_w_gate_2"][n]) for n in range(2)]
    for n, (p, proj, gate) in enumerate(ple):
        arrays[f"p{n}"] = _turned(p)
        arrays[f"ple{n}_proj"] = np.ascontiguousarray(
            _tiles(proj).reshape(2, 4, P, 2 * P).transpose(0, 2, 1, 3)).reshape(2, P, SLOT)
        arrays[f"ple{n}_gate"] = _tiles(gate)

    w_in = a["w_in"][0]
    panel = lambda c, n=1: _tiles(w_in[:, c:c + n * P])
    arrays["mix_first"] = np.concatenate([panel(1152), panel(512), panel(640, 4), panel(0, 4)])
    arrays["hgrn"] = np.stack([panel(1736, 4), panel(1224, 4), panel(2248, 4), panel(2760, 4)], 1).reshape(16, P, D)
    both = np.concatenate([_tiles(a["w_br_a"][0]), _tiles(a["w_br_b"][0])], 2)
    arrays["merge"] = np.stack([panel(3272, 8), panel(4296, 8), both], 1).reshape(24, P, D)
    arrays["w_out"] = _tiles(a["w_out"][0])
    w_uk, w_uv = a["w_uk"][0], a["w_uv"][0]
    arrays["w_uk"] = np.ascontiguousarray(w_uk.reshape(4, 2, P, 64).transpose(1, 3, 0, 2)).reshape(P, 4 * P)
    arrays["w_uv"] = np.ascontiguousarray(w_uv.transpose(1, 0, 2)).reshape(P, 4 * P)
    vec("kidx_norm_g", np.concatenate([a["kidx_norm_g"][0]] * 2))
    vec("kv_norm_g", a["kv_norm_g"][0])
    vec("hgrn_norm_g", a["hgrn_norm_g"][0])
    vec("b_gate", a["b_gate"][0])
    for n in range(2):
        vec(f"hgrn_lb{n}", a["hgrn_lb"][n])
    t = np.arange(P)
    masks = [(t[:, None] // (2 * L) == t[None, :] // (2 * L)) & (t[:, None] % (2 * L) < L) & (t[None, :] % (2 * L) >= L)
             for L in (P >> l for l in range(1, LEVELS + 1))]
    arrays["level_masks"] = np.concatenate(masks, 1).astype(np.float32)

    for n, (table, name, pos) in enumerate(((a["rel_bias"], "iota", np.arange(T, dtype=np.int32)),
                                            (a["rel_bias_table_2"], "pos", a["positions_2"][0]))):
        before = np.concatenate([np.zeros_like(table[:1]), table[:-1]])
        arrays[f"table{n}"] = np.tile(np.concatenate([table, before], 1), (4, 1))
        arrays[name] = pos.reshape(1, T)
        arrays[name + "_rows"] = np.ascontiguousarray(pos.reshape(P, 4).T)
    arrays["lam"] = np.concatenate([a[n][0] for n in ("a_lam_q1_2", "a_lam_k1_2", "a_lam_q2_2", "a_lam_k2_2")])[None]

    qkv = _tiles(a["a_w_qkv_2"][0]).reshape(3, HEADS, P, D)
    arrays["diff"] = np.ascontiguousarray(qkv.transpose(1, 0, 2, 3)).reshape(3 * HEADS, P, D)
    arrays["a_w_o"] = _tiles(a["a_w_o_2"][0])
    vec("a_q_norm", np.concatenate([a["a_q_norm_2"][0]] * 2))
    vec("a_k_norm", np.concatenate([a["a_k_norm_2"][0]] * 2))
    vec("a_sub_norm", a["a_sub_norm_2"][0])
    vec("kv_norm", a["kv_norm_2"])
    vec("ckv_norm", a["ckv_norm_2"])
    vec("k_nope_norm", a["k_nope_norm_2"])
    vec("k_pe_norm", np.concatenate([a["k_pe_norm_2"]] * 2))
    vec("b_cq_norm", a["b_cq_norm_2"][0])
    vec("b_q_nope_norm", a["b_q_nope_norm_2"][0])
    vec("b_q_pe_norm", np.concatenate([a["b_q_pe_norm_2"][0]] * 2))
    dkv = a["w_dkv_2"]
    arrays["w_dkv"] = _tiles(np.concatenate([dkv, dkv[:, 256:]], 1))
    arrays["w_dq"] = _tiles(a["b_w_dq_2"][0])
    uq = a["b_w_uq_2"][0].reshape(512, 16, 192)
    q_nope = _tiles(np.ascontiguousarray(uq[:, :, 0:P]).reshape(512, 16 * P))
    kv = _tiles(a["w_ukv_2"]).reshape(16, 2, P, 2 * P)
    arrays["mla"] = np.concatenate([q_nope, kv[:, 0], kv[:, 1]], 2)
    arrays["mla_pe"] = _tiles(np.ascontiguousarray(uq[:, :, P:]).reshape(512, 16 * 64))
    for n in range(2):
        arrays[f"b_w_o{n}"] = _tiles(a["b_w_o_2"][0][n * D:(n + 1) * D])

    arrays["vecs"] = np.concatenate(cols, axis=1)
    nc = bacc.Bacc("TRN2", target_bir_lowering=False, num_devices=1)
    dram = {n: nc.dram_tensor("in_" + n, v.shape, mybir.dt.from_np(v.dtype), kind="ExternalInput").ap()
            for n, v in arrays.items()}
    dram["out"] = nc.dram_tensor("out", (P, KD * T), F32, kind="ExternalOutput").ap()
    dram["strip"] = nc.dram_tensor("strip", (P * HEADS, T), F32).ap()
    dram["bias"] = nc.dram_tensor("bias", (T * HEADS, T), F32).ap()
    program(nc, dram, V)
    r = run_bass_kernel_spmd(nc, [{"in_" + n: v for n, v in arrays.items()}], core_ids=[0])
    out = r.results[0]["out"]
    return np.ascontiguousarray(out.reshape(P, KD, T).transpose(2, 1, 0)).reshape(1, T, D)
```
